# Optimizing a Trainium2 kernel written in Bass

```python
import math
import jax, jax.numpy as jnp
from jax import lax
import numpy as np

D_MODEL = 1024
BATCH = 1
SEQ = 1024
DEPTH = 1
DEC_BATCH = 1
DEC_SEQ = 64
PAST_LEN = 512

CHUNK = 64
EPS = 1e-6
POOL_WINDOWS = (2, 4, 8, 16)
N_POOL_GROUPS = 4
POOL_WIDTH = D_MODEL
POOL_GROUP = POOL_WIDTH // N_POOL_GROUPS
POOL_STATE = max(POOL_WINDOWS) - 1
SSM_EXPAND = 2
D_INNER = SSM_EXPAND * D_MODEL
SSM_HEAD_DIM = 64
N_SSM_HEADS = D_INNER // SSM_HEAD_DIM
N_SSM_GROUPS = 4
HEADS_PER_GROUP = N_SSM_HEADS // N_SSM_GROUPS
D_STATE = 128
CONV_WIDTH = 4
CONV_DIM = D_INNER + 2 * N_SSM_GROUPS * D_STATE
SSD_BLOCK = CHUNK
D_FF = ((8 * D_MODEL // 3 + 255) // 256) * 256
P_END = POOL_WIDTH
Z_END = P_END + D_INNER
XBC_END = Z_END + CONV_DIM
DT_END = XBC_END + N_SSM_HEADS
GA_END = DT_END + D_MODEL
N_IN = GA_END + D_MODEL

kernel_name = "pool_ssd_gated_hybrid_stream_step"

def _rmsnorm(x, w):
    xf = x.astype(jnp.float32)
    y = xf * lax.rsqrt(jnp.mean(xf * xf, axis=-1, keepdims=True) + EPS)
    return (y * w.astype(jnp.float32)).astype(x.dtype)

def _pool_mixer(p, p_hist, pos0, w_group, pool_scale):
    b, L, _ = p.shape
    full = jnp.concatenate([p_hist.astype(p.dtype), p], axis=1)
    pf = full.astype(jnp.float32)
    csum = jnp.concatenate([jnp.zeros((b, 1, POOL_WIDTH), jnp.float32), jnp.cumsum(pf, axis=1)], axis=1)
    end = csum[:, POOL_STATE + 1:]
    pos = pos0 + jnp.arange(L)
    outs = []
    for g, w in enumerate(POOL_WINDOWS):
        sl = slice(g * POOL_GROUP, (g + 1) * POOL_GROUP)
        start = csum[:, POOL_STATE + 1 - w: POOL_STATE + 1 - w + L, sl]
        cnt = jnp.minimum(pos + 1, w).astype(jnp.float32)[None, :, None]
        outs.append((end[..., sl] - start) / cnt - pf[:, POOL_STATE:, sl])
    m = jnp.stack(outs, axis=2)
    y = jnp.einsum('blgc,gcd->blgd', m, w_group.astype(jnp.float32)).reshape(b, L, POOL_WIDTH)
    y = y * pool_scale.astype(jnp.float32)
    return y.astype(p.dtype), full[:, -POOL_STATE:]

def _causal_conv(u, u_hist, w, bias):
    full = jnp.concatenate([u_hist.astype(u.dtype), u], axis=1)
    y = lax.conv_general_dilated(full, w[:, None, :].astype(u.dtype), (1,), 'VALID',
                                 dimension_numbers=('NWC', 'WIO', 'NWC'),
                                 feature_group_count=CONV_DIM)
    return y + bias, full[:, -(CONV_WIDTH - 1):]

def _ssd_scan(x, dt, A, Bm, Cm, h0, block):
    b, L = x.shape[:2]
    nc = L // block
    G, R, P, N = N_SSM_GROUPS, HEADS_PER_GROUP, SSM_HEAD_DIM, D_STATE
    f32 = jnp.float32
    x = x.reshape(b, nc, block, G, R, P).astype(f32)
    dt = dt.reshape(b, nc, block, G, R)
    Bm = Bm.reshape(b, nc, block, G, N).astype(f32)
    Cm = Cm.reshape(b, nc, block, G, N).astype(f32)
    acs = jnp.cumsum(dt * A.reshape(G, R), axis=2)
    mask = jnp.tril(jnp.ones((block, block), bool))[:, :, None, None]
    seg = acs[:, :, :, None] - acs[:, :, None, :]
    decay = jnp.exp(jnp.where(mask, seg, -jnp.inf))
    cb = jnp.einsum('bclgn,bcsgn->bclsg', Cm, Bm)
    y_diag = jnp.einsum('bclsg,bclsgr,bcsgr,bcsgrp->bclgrp', cb, decay, dt, x)
    decay_to_end = jnp.exp(acs[:, :, -1:] - acs)
    states = jnp.einsum('bclgn,bclgr,bclgrp->bcgrpn', Bm, decay_to_end * dt, x)
    block_decay = jnp.exp(acs[:, :, -1])

    def step(h, inp):
        s, d = inp
        return d[..., None, None] * h + s, h

    h_init = h0.reshape(b, G, R, P, N).astype(f32)
    h_last, h_prev = lax.scan(step, h_init, (jnp.moveaxis(states, 1, 0), jnp.moveaxis(block_decay, 1, 0)))
    h_prev = jnp.moveaxis(h_prev, 0, 1)
    y_off = jnp.einsum('bclgn,bcgrpn,bclgr->bclgrp', Cm, h_prev, jnp.exp(acs))
    y = (y_diag + y_off).reshape(b, L, N_SSM_HEADS, P)
    return y, h_last.reshape(b, N_SSM_HEADS, P, N)

def _ssd_mixer(z, xbc, dt_raw, conv_hist, h0, block, conv_w, conv_b, dt_bias, a_log, d_skip, norm_w):
    b, L, _ = z.shape
    xbc_c, new_conv = _causal_conv(xbc, conv_hist, conv_w, conv_b)
    xbc_c = jax.nn.silu(xbc_c)
    xs = xbc_c[..., :D_INNER].reshape(b, L, N_SSM_HEADS, SSM_HEAD_DIM)
    Bm = xbc_c[..., D_INNER:D_INNER + N_SSM_GROUPS * D_STATE].reshape(b, L, N_SSM_GROUPS, D_STATE)
    Cm = xbc_c[..., D_INNER + N_SSM_GROUPS * D_STATE:].reshape(b, L, N_SSM_GROUPS, D_STATE)
    dt = jax.nn.softplus(dt_raw.astype(jnp.float32) + dt_bias.astype(jnp.float32))
    A = -jnp.exp(a_log.astype(jnp.float32))
    y, h_last = _ssd_scan(xs, dt, A, Bm, Cm, h0, block)
    y = y + d_skip.astype(jnp.float32)[:, None] * xs.astype(jnp.float32)
    y = y.reshape(b, L, D_INNER) * jax.nn.silu(z.astype(jnp.float32))
    yg = y.reshape(b, L, N_SSM_GROUPS, D_INNER // N_SSM_GROUPS)
    yg = yg * lax.rsqrt(jnp.mean(yg * yg, axis=-1, keepdims=True) + EPS)
    y = yg.reshape(b, L, D_INNER) * norm_w.astype(jnp.float32)
    return y.astype(z.dtype), new_conv, h_last.astype(h0.dtype)

def _layer(x, c, pool_hist, conv_hist, ssm_h, pos0, block,
           w_ada, b_ada, norm1_w, norm2_w, w_in, pool_group_w, pool_scale, conv_w, conv_b,
           dt_bias, a_log, d_skip, ssm_norm_w, w_branch_a, w_branch_b, w_out,
           w_ffn_gate, w_ffn_up, w_ffn_down):
    mod = jax.nn.silu(c) @ w_ada + b_ada
    shift1, scale1, gate1, shift2, scale2, gate2 = jnp.split(mod[:, None, :], 6, axis=-1)
    h = _rmsnorm(x, norm1_w) * (1 + scale1) + shift1
    u = h @ w_in
    p = u[..., :P_END]
    z = u[..., P_END:Z_END]
    xbc = u[..., Z_END:XBC_END]
    dt_raw = u[..., XBC_END:DT_END]
    g_a = u[..., DT_END:GA_END]
    g_b = u[..., GA_END:]
    a_out, new_pool = _pool_mixer(p, pool_hist, pos0, pool_group_w, pool_scale)
    b_out, new_conv, new_ssm = _ssd_mixer(z, xbc, dt_raw, conv_hist, ssm_h, block, conv_w, conv_b,
                                          dt_bias, a_log, d_skip, ssm_norm_w)
    merged = jax.nn.sigmoid(g_a) * (a_out @ w_branch_a) + jax.nn.sigmoid(g_b) * (b_out @ w_branch_b)
    x = x + gate1 * (merged @ w_out)
    h2 = _rmsnorm(x, norm2_w) * (1 + scale2) + shift2
    f = (jax.nn.silu(h2 @ w_ffn_gate) * (h2 @ w_ffn_up)) @ w_ffn_down
    x = x + gate2 * f
    return x, new_pool, new_conv, new_ssm

def setup_inputs(seed: int = 0) -> dict:
    key = jax.random.key(seed)
    ks = jax.random.split(key, 32)
    f32 = jnp.float32

    def nrm(k, shape, scale):
        return jax.random.normal(k, shape, f32) * scale

    L = DEPTH
    dt_init = jnp.exp(jax.random.uniform(ks[16], (L, N_SSM_HEADS), f32, math.log(1e-3), math.log(1e-1)))
    return {
        "x_prompt": nrm(ks[0], (BATCH, SEQ, D_MODEL), 1.0),
        "x_sample": nrm(ks[1], (DEC_BATCH, DEC_SEQ, D_MODEL), 1.0),
        "c_prompt": nrm(ks[2], (BATCH, D_MODEL), 1.0),
        "c_sample": nrm(ks[3], (DEC_BATCH, D_MODEL), 1.0),
        "state_pool": nrm(ks[4], (L, DEC_BATCH, POOL_STATE, POOL_WIDTH), 1.0),
        "state_conv": nrm(ks[5], (L, DEC_BATCH, CONV_WIDTH - 1, CONV_DIM), 1.0),
        "state_ssm": nrm(ks[6], (L, DEC_BATCH, N_SSM_HEADS, SSM_HEAD_DIM, D_STATE), 0.1),
        "w_ada": nrm(ks[7], (L, D_MODEL, 6 * D_MODEL), 0.5 * D_MODEL ** -0.5),
        "b_ada": nrm(ks[8], (L, 6 * D_MODEL), 0.02),
        "norm1_w": 1.0 + nrm(ks[9], (L, D_MODEL), 0.02),
        "norm2_w": 1.0 + nrm(ks[10], (L, D_MODEL), 0.02),
        "w_in": nrm(ks[11], (L, D_MODEL, N_IN), D_MODEL ** -0.5),
        "pool_group_w": nrm(ks[12], (L, N_POOL_GROUPS, POOL_GROUP, POOL_GROUP), POOL_GROUP ** -0.5),
        "pool_scale": 1.0 + nrm(ks[13], (L, POOL_WIDTH), 0.1),
        "conv_w": nrm(ks[14], (L, CONV_WIDTH, CONV_DIM), CONV_WIDTH ** -0.5),
        "conv_b": nrm(ks[15], (L, CONV_DIM), 0.02),
        "dt_bias": dt_init + jnp.log(-jnp.expm1(-dt_init)),
        "a_log": jnp.log(jax.random.uniform(ks[17], (L, N_SSM_HEADS), f32, 1.0, 16.0)),
        "d_skip": 1.0 + nrm(ks[18], (L, N_SSM_HEADS), 0.1),
        "ssm_norm_w": 1.0 + nrm(ks[19], (L, D_INNER), 0.02),
        "w_branch_a": nrm(ks[20], (L, POOL_WIDTH, D_MODEL), POOL_WIDTH ** -0.5),
        "w_branch_b": nrm(ks[21], (L, D_INNER, D_MODEL), D_INNER ** -0.5),
        "w_out": nrm(ks[22], (L, D_MODEL, D_MODEL), D_MODEL ** -0.5),
        "w_ffn_gate": nrm(ks[23], (L, D_MODEL, D_FF), D_MODEL ** -0.5),
        "w_ffn_up": nrm(ks[24], (L, D_MODEL, D_FF), D_MODEL ** -0.5),
        "w_ffn_down": nrm(ks[25], (L, D_FF, D_MODEL), D_FF ** -0.5),
        "final_norm_w": 1.0 + nrm(ks[26], (D_MODEL,), 0.02),
    }

def reference(x_prompt, x_sample, c_prompt, c_sample, state_pool, state_conv, state_ssm,
              w_ada, b_ada, norm1_w, norm2_w, w_in, pool_group_w, pool_scale, conv_w, conv_b,
              dt_bias, a_log, d_skip, ssm_norm_w, w_branch_a, w_branch_b, w_out,
              w_ffn_gate, w_ffn_up, w_ffn_down, final_norm_w):
    xp, xs = x_prompt, x_sample
    bp = xp.shape[0]
    pool_p, conv_p, ssm_p, pool_s, conv_s, ssm_s = [], [], [], [], [], []
    for l in range(DEPTH):
        params = (w_ada[l], b_ada[l], norm1_w[l], norm2_w[l], w_in[l], pool_group_w[l], pool_scale[l],
                  conv_w[l], conv_b[l], dt_bias[l], a_log[l], d_skip[l], ssm_norm_w[l],
                  w_branch_a[l], w_branch_b[l], w_out[l], w_ffn_gate[l], w_ffn_up[l], w_ffn_down[l])
        xp, sp_, cp_, hp_ = _layer(
            xp, c_prompt,
            jnp.zeros((bp, POOL_STATE, POOL_WIDTH), xp.dtype),
            jnp.zeros((bp, CONV_WIDTH - 1, CONV_DIM), xp.dtype),
            jnp.zeros((bp, N_SSM_HEADS, SSM_HEAD_DIM, D_STATE), state_ssm.dtype),
            0, SSD_BLOCK, *params)
        xs, ss_, cs_, hs_ = _layer(
            xs, c_sample, state_pool[l], state_conv[l], state_ssm[l],
            PAST_LEN, xs.shape[1], *params)
        pool_p.append(sp_); conv_p.append(cp_); ssm_p.append(hp_)
        pool_s.append(ss_); conv_s.append(cs_); ssm_s.append(hs_)
    y_prompt = _rmsnorm(xp, final_norm_w)
    y_sample = _rmsnorm(xs, final_norm_w)
    return (y_prompt, y_sample,
            jnp.stack(pool_p), jnp.stack(conv_p), jnp.stack(ssm_p),
            jnp.stack(pool_s), jnp.stack(conv_s), jnp.stack(ssm_s))


_drawn_inputs = setup_inputs


def setup_inputs(seed=0):
    import zlib

    import numpy as np

    out = dict(_drawn_inputs(seed))
    spreads = {}
    factors = {'state_pool': 4.646,
     'norm2_w': 8.0,
     'pool_scale': 3.433,
     'd_skip': 5.312,
     'ssm_norm_w': 8.0,
     'final_norm_w': 2.776}
    for name, (base, spread) in spreads.items():
        noise = np.random.default_rng([zlib.crc32(name.encode()), seed]).standard_normal(out[name].shape)
        drawn = base * np.exp(spread * noise) if base else spread * noise
        out[name] = __import__('jax').numpy.asarray(drawn.astype(out[name].dtype))
    for name, factor in factors.items():
        out[name] = (out[name] * factor).astype(out[name].dtype)
    return out
```

```python
import concourse.bass as bass
from concourse import mybir

F32 = mybir.dt.float32
F32R = mybir.dt.float32r
ALU = mybir.AluOpType
ACT = mybir.ActivationFunctionType
ds = bass.ds

P = 128
D = 1024
KT = D // P
SEQ, DEC = 1024, 64
T = SEQ + DEC
CH = 128
NCH = SEQ // CH + 1
HEADS, GROUPS, HPG, HD, NS = 32, 4, 8, 64, 128
DIN = 2 * D
CONV = DIN + 2 * GROUPS * NS
CT = CONV // P
PW = 15
DFF = 2816
FG = DFF // P // 2
EPS = 1e-6
COL_Z, COL_XBC, COL_DT, COL_GATES = D, D + DIN, D + DIN + CONV, D + DIN + CONV + HEADS
THIRD = 364
SUBS = [(0, THIRD), (THIRD, THIRD), (2 * THIRD, T - 2 * THIRD)]
SHIFT1, SCALE1, GATE1, SHIFT2, SCALE2, GATE2 = [i * KT for i in range(6)]
PASSES = [(0, 0), (0, 1), (1, 0)]


def build(nc, A, O):
    base = 16512
    plan = {}

    def at(name, shape, dt, offset):
        n = 1
        for s in shape[1:]:
            n *= s
        plan[name] = (offset, offset + 4 * n)
        return nc.alloc_sbuf_tensor_at(name, shape, dt, offset=offset)

    cursor = [base]
    ADA_DVE = 5

    def keep(name, shape, dt=F32):
        t = at(name, shape, dt, cursor[0])
        cursor[0] = (plan[name][1] + 31) // 32 * 32
        return t

    ident = keep("ident", [P, P])
    upper = keep("upper", [P, P])
    ones = keep("ones", [P, P])
    cols_conv = keep("cols_conv", [P, 5 * CT])
    cols_vec = keep("cols_vec", [P, 104])
    cols_hist = keep("cols_hist", [P, 3 * CT])
    cols_pool = keep("cols_pool", [P, PW * KT])
    silu_c = keep("silu_c", [P, KT, 2])
    mods = keep("mods", [P, 48, 2])
    gain = keep("gain", [P, 2, 2, KT])
    bc_head = keep("bc_head", [P, 3, HEADS])
    half = keep("half", [P, 2])
    inv_pos = keep("inv_pos", [P, PW])
    small = keep("small", [P, 8])
    conv_tail = keep("conv_tail", [P, 2, 3, CT])
    dt_tab = keep("dt_tab", [P, NCH, HEADS])
    nacs_tab = keep("nacs_tab", [P, NCH, HEADS])
    eacs_tab = keep("eacs_tab", [P, NCH, HEADS])
    dend_tab = keep("dend_tab", [P, NCH, HEADS])
    bdec_tab = keep("bdec_tab", [P, NCH, HEADS])
    w_raw = [keep(f"w_raw{i}", [P, 1024]) for i in range(2)]
    w_split = [[keep(f"w_{n}{i}", [P, 1024], F32R) for n in ("hi", "lo")] for i in range(2)]
    RA = cursor[0]
    RB = RA + 2 * KT * T * 4
    RC = RB + 2 * KT * T * 4
    REND = RC + KT * T * 4
    act_a = [at(f"act_a_{n}", [P, KT, T], F32R, RA + i * KT * T * 4) for i, n in enumerate(("hi", "lo"))]
    act_b = [at(f"act_b_{n}", [P, KT, T], F32R, RB + i * KT * T * 4) for i, n in enumerate(("hi", "lo"))]
    acc = at("acc", [P, KT, T], F32, RC)

    def region(start, end, *items):
        out, o = [], start
        for name, shape, dt in items:
            out.append(at(name, shape, dt, o))
            o = (plan[name][1] + 31) // 32 * 32
        assert o <= end, (items[0][0], o, end)
        return out

    (rows_conv, rows_vec, rows_hist, rows_pool, ada0, ada1, xin0, xin1, junk, hf0, hf1, z0, z1, raw0, raw1, cv0, cv1,
     wdt_raw, wdt_hi, wdt_lo, dt_row, dt_in, dt_e, dt_s, dt_q, dt_p) = region(
        RB, REND,
        ("rows_conv", [5 * CT, P], F32), ("rows_vec", [104, P], F32), ("rows_hist", [3 * CT, P], F32),
        ("rows_pool", [PW * KT, P], F32),
        ("ada0", [P, KT, 256], F32), ("ada1", [P, KT, 256], F32),
        ("xin0", [P, D], F32), ("xin1", [P, D], F32), ("junk", [P, D], F32),
        ("hf0", [P, KT, P], F32), ("hf1", [P, KT, P], F32),
        ("zb0", [P, T + DEC], F32), ("zb1", [P, T + DEC], F32),
        ("raw0", [P, 1160], F32), ("raw1", [P, 1160], F32), ("cv0", [P, T + 3 + DEC], F32), ("cv1", [P, T + 3 + DEC], F32),
        ("wdt_raw", [P, KT * HEADS], F32), ("wdt_hi", [P, KT * HEADS], F32R), ("wdt_lo", [P, KT * HEADS], F32R),
        ("dt_row", [HEADS, T], F32), ("dt_in", [P, NCH, HEADS], F32), ("dt_e", [P, NCH, HEADS], F32),
        ("dt_s", [P, NCH, HEADS], F32), ("dt_q", [P, NCH, HEADS], F32), ("dt_p", [P, NCH, HEADS], F32))
    o_end = (plan["dt_p"][1] + 31) // 32 * 32
    (acs_row,) = region(plan["hf0"][0], plan["hf1"][1], ("acs_row", [HEADS, NCH * CH], F32))
    (ada_sum,) = region(o_end, REND, ("ada_sum", [P, ADA_DVE, 2, 256], F32))
    ada, xin, hf, zb, raw, cv = [ada0, ada1], [xin0, xin1], [hf0, hf1], [z0, z1], [raw0, raw1], [cv0, cv1]
    wdt = [wdt_hi, wdt_lo]

    ada_first = region(RA, RB, *[(f"ada_first{k}", [P, KT, 256], F32) for k in range(8)])

    s = region(
        RB, REND,
        *[(f"xs_in{i}", [P, 4, CH], F32) for i in range(3)], *[(f"bc_in{i}", [P, 2, CH], F32) for i in range(3)],
        *[(f"z_in{i}", [P, 4, CH], F32) for i in range(3)], *[(f"acs_in{i}", [P, HPG, CH], F32) for i in range(3)],
        ("gp0", [P, T], F32), ("gp1", [P, T], F32),
        ("x_dt", [P, HPG, HD], F32), ("x_end", [P, HPG, HD], F32), ("b_tok", [P, NS], F32), 
        ("decay", [P, HPG, CH], F32), ("mix", [P, HPG, CH], F32), ("state", [P, HPG, HD], F32),
        ("skip", [P, HPG, HD], F32), ("y_tok", [P, HPG, HD], F32), ("yg0", [P, 4, CH], F32), ("yg1", [P, 4, CH], F32),
        ("yg2", [P, 4, CH], F32),
        ("state_in", [P, 4, NS], F32), ("state_out0", [P, 4, NS], F32), ("state_out1", [P, 4, NS], F32))
    xs_in, bc_in, z_in, acs_in, gp = s[0:3], s[3:6], s[6:9], s[9:12], s[12:14]
    x_dt, x_end, b_tok, decay, mix, state, skip, y_tok = s[14:22]
    yg, state_in, state_out = s[22:25], s[25], s[26:28]

    y_in0, y_in1, ysq, rms_v, rms_g, tail_rows = region(
        RB, RC, ("y_in0", [P, 4, T], F32), ("y_in1", [P, 4, T], F32), ("ysq", [P, 4, T], F32), ("rms_v", [P, NCH], F32),
        ("rms_g", [P, NCH], F32), ("tail_rows", [3 * CT, 2, P], F32))
    y_in = [y_in0, y_in1]
    pw_ = SEQ + DEC + 2 * PW
    pl_in0, pl_in1, pl_s0, pl_s1, pm_hi, pm_lo, pool_f, pool_tail, pool_rows, a_val0, a_val1 = region(
        RA, RB, ("pl_in0", [P, pw_], F32), ("pl_in1", [P, pw_], F32), ("pl_s0", [P, pw_], F32), ("pl_s1", [P, pw_], F32),
        ("pm_hi", [P, 2, T], F32R), ("pm_lo", [P, 2, T], F32R), ("pool_f", [P, T], F32),
        ("pool_tail", [P, 2, PW, KT], F32), ("pool_rows", [PW * KT, 2, P], F32), ("a_val0", [P, T], F32), ("a_val1", [P, T], F32))
    pl_in, a_val = [pl_in0, pl_in1], [a_val0, a_val1]
    ga0, ga1, gb0, gb1, mg_t = region(
        RA, RB, *[(n, [P, T], F32) for n in ("ga0", "ga1", "gb0", "gb1")], ("mg_t", [P, T], F32))
    gates = [[ga0, gb0], [ga1, gb1]]
    (st0, st1, x2_0, x2_1, xr0, xr1, g2_junk, xn0, xn1, h20, h21) = region(
        RA, RB, *[(n, [P, KT, P], F32) for n in ("st0", "st1", "x2_0", "x2_1", "xr0", "xr1", "g2_junk", "xn0", "xn1",
                                                  "h20", "h21")])
    st, x2, xr, xn, h2 = [st0, st1], [x2_0, x2_1], [xr0, xr1], [xn0, xn1], [h20, h21]
    ff = region(RA, RB, *[(f"f_{n}{i}", [P, 2, T], F32R) for i in range(1) for n in ("hi", "lo")],
                ("silu_g", [P, T], F32), ("f_val", [P, T], F32))
    f_split = ff[0:2]
    silu_g, f_val = ff[2], ff[3]
    (ft0, ft1, fx0, fx1, fr0, fr1, fjunk, fo0, fo1, final_w) = region(
        RB, RC, *[(n, [P, KT, P], F32) for n in ("ft0", "ft1", "fx0", "fx1", "fr0", "fr1", "fjunk", "fo0", "fo1",
                                                  "final_w")])
    ft, fx, fr, fo = [ft0, ft1], [fx0, fx1], [fr0, fr1], [fo0, fo1]

    PS = nc.alloc_psum_tensor("PS", [P, 8, 512], F32)

    def dram(name, shape):
        return nc.dram_tensor(name, shape, F32, kind="Internal").ap()

    xs_c = dram("xs_c", (GROUPS * NCH, 4, P, CH))
    bc_c = dram("bc_c", (2, GROUPS * NCH, P, CH))
    z_c = dram("z_c", (GROUPS * NCH, 4, P, CH))
    acs_c = dram("acs_c", (GROUPS * NCH, HPG, CH))
    gp_s = dram("gp_s", (3 * KT, P, T))
    y_c = dram("y_c", (GROUPS * NCH, 4, P, CH))
    x2_s = dram("x2_s", (NCH, P, D))

    def S(name):
        return nc.alloc_semaphore(name)


    rows_in, consts, cols_ready, c_ready = S("rows_in"), S("consts"), S("cols_ready"), S("silu_c_ready")
    rows_t = S("rows_transposed")
    w_in_ = [S(f"w_landed{i}") for i in range(2)]
    hi_ready, lo_ready = S("w_hi_ready"), S("w_lo_ready")
    ada_in = [S(f"ada_landed{i}") for i in range(2)]
    ada_used, mods_mm, mods_ready = S("ada_summed"), S("mods_mm"), S("mods_ready")
    wdt_in, wdt_h, wdt_l = S("wdt_landed"), S("wdt_hi_ready"), S("wdt_lo_ready")
    dt_mm, dt_copied, dt_tok, dt_vec, dt_act = S("dt_mm"), S("dt_copied"), S("dt_tok"), S("dt_vec"), S("dt_act")
    dt_cum, acs_out = S("dt_cumsum"), S("acs_stored")
    mm, mm_free = {}, {}
    for ph in ("z", "xbc", "ssd", "brb", "pool", "bra", "out", "ffn"):
        mm[ph], mm_free[ph] = S(f"mm_{ph}"), S(f"bank_free_{ph}")
    z_store = [S(f"z_stored{i}") for i in range(2)]
    raw_hist = S("raw_hist")
    cv_step, cv_silu, cv_store = S("conv_step"), S("conv_silu"), [S(f"conv_stored{i}") for i in range(2)]
    chunk_in = [S(f"chunk_landed{i}") for i in range(3)]
    gp_store = [S(f"gp_stored{i}") for i in range(2)]
    y_store = [S(f"y_stored{i}") for i in range(3)]
    (ssd_a, ssd_b, ssd_c, decay_ready, masked, mask_turn, v_x, v_skip, v_b, v_xend, v_mix, v_y0, v_y1, y_ready, v_s0, state_ready,
     yg_ready, edge_t, edge_v, st_in) = [S(n) for n in (
         "ssd_tokens", "ssd_products", "ssd_turned", "decay_ready", "acs_masked", "mask_turn", "x_dt_ready", "skip_ready", "b_tok_ready",
         "x_end_ready", "mix_ready", "y_off_scaled", "y_summed", "y_ready", "state_decayed",
         "state_ready", "yg_ready", "edge_turned", "edge_copied", "state_landed")]
    edge_store = [S(f"state_stored{i}") for i in range(2)]
    y_back = [S(f"y_landed{i}") for i in range(2)]
    ysq_ready, gs_mm, rms_vec, rms_pow, rms_wide, yn_ready, yb_hi, yb_lo = [S(n) for n in (
        "ysq_ready", "group_sum", "group_variance", "group_rms", "rms_spread", "y_normed", "y_hi", "y_lo")]
    tails_t, tails_v, tails_out = S("tails_turned"), S("tails_copied"), S("tails_stored")
    pl_landed = [S(f"pool_landed{i}") for i in range(2)]
    pl_vec, pm_h, pm_l, av, ab_hi, ab_lo, pl_set = [S(n) for n in (
        "pool_vec", "pooled_hi", "pooled_lo", "a_val_ready", "a_hi", "a_lo", "pool_set")]
    ptail_t, ptail_v, ptail_out = S("pool_tails_turned"), S("pool_tails_copied"), S("pool_tails_stored")
    gate_in = [S(f"gate_landed{i}") for i in range(2)]
    gate_tanh, mg_vec, mg_hi, mg_lo = S("gate_tanh"), S("merge_vec"), S("merged_hi"), S("merged_lo")
    f_silu, f_hi, f_lo = S("ffn_silu"), S("ffn_hi"), S("ffn_lo")
    y_add = S("ffn_added")
    out_sem, x2_out = [S(f"y_out{i}") for i in range(2)], [S(f"x2_stored{i}") for i in range(2)]

    class Norm:
        def __init__(self, n):
            self.landed = [S(f"{n}_landed{i}") for i in range(2)]
            (self.staged, self.turned_in, self.added, self.squared, self.var, self.rms, self.scaled, self.turned,
             self.modulated, self.hi, self.lo) = [S(f"{n}_{k}") for k in (
                 "staged", "turned_in", "added", "squared", "var", "rms", "scaled", "turned", "modulated", "hi", "lo")]

    n1, n2, n3 = Norm("norm1"), Norm("norm2"), Norm("norm3")
    fw_in = S("final_w_landed")

    def kmaj(w):
        return w.rearrange("(k p) n -> p k n", p=P)

    x_p, x_s = A["x_prompt"][0], A["x_sample"][0]
    yo_p, yo_s = O[0][0], O[1][0]
    win, wada = kmaj(A["w_in"][0]), kmaj(A["w_ada"][0])
    U_SSD, U_B = 40, 64
    U_POOL = U_B + 16
    U_A = U_POOL + 2
    U_OUT = U_A + 8
    U_FFN = U_OUT + 8
    U_END = U_FFN + 6 * FG
    FFN_SUBS, FFN_DVE = 36 * FG, 30 * FG
    DV_DTA, DV_TAB, N_ROWS, N_MEMSET = 19, 26, 14, 3 + PW + 1 + 6
    POLY = [1.0 / (2 * k + 1) for k in range(9)]

    def bank(b):
        return PS[:, b, :]

    def banks2(b, n=P):
        return PS[:, b:b + 2, :].rearrange("p b (f l) -> p (b f) l", l=P)

    def hb(tab, c, g):
        return tab[:, c, :][:, ds(g * HPG, HPG)].unsqueeze(2).broadcast_to([P, HPG, HD])

    PL_DONE = []
    for j in range(KT):
        PL_DONE.append((PL_DONE[-1] if j else 0) + 3 + (j // 2 + 1) + 4)

    blk = nc.Block()
    with blk as block:
        @block.sync
        def _(sp):
            def load_unit(u, v, src, first=False):
                if not first:
                    sp.wait_ge(lo_ready, u - 1)
                sp.dma_start(w_raw[v][:, :].rearrange("p (k n) -> p k n", n=src.shape[-1]), src).then_inc(w_in_[v], 16)

            def vec(w):
                return w.rearrange("(t c) -> t c", c=P)

            rows = [(rows_conv[0:4 * CT, :], A["conv_w"][0].rearrange("k (t c) -> (k t) c", c=P)),
                    (rows_conv[4 * CT:5 * CT, :], vec(A["conv_b"][0])),
                    (rows_vec[0:48, :], vec(A["b_ada"][0])), (rows_vec[48:56, :], vec(A["norm1_w"][0])),
                    (rows_vec[56:64, :], vec(A["norm2_w"][0])), (rows_vec[64:72, :], vec(A["pool_scale"][0])),
                    (rows_vec[72:88, :], vec(A["ssm_norm_w"][0])), (rows_vec[88:96, :], vec(A["c_prompt"][0])),
                    (rows_vec[96:104, :], vec(A["c_sample"][0])),
                    (rows_hist[:, :], A["state_conv"][0, 0].rearrange("k (t c) -> (k t) c", c=P)),
                    (rows_pool[:, :], A["state_pool"][0, 0].rearrange("k (t c) -> (k t) c", c=P)),
                    (bc_head[:, 0, :], A["dt_bias"][0].partition_broadcast(P)),
                    (bc_head[:, 1, :], A["a_log"][0].partition_broadcast(P)),
                    (bc_head[:, 2, :], A["d_skip"][0].partition_broadcast(P))]
            assert len(rows) == N_ROWS
            for dst, src in rows:
                sp.dma_start(dst, src).then_inc(rows_in, 16)
            for k in range(8):
                sp.dma_start(ada_first[k][:, :, :], wada[:, :, k * 256:(k + 1) * 256]).then_inc(ada_in[k >= ADA_DVE], 16)
                if k < 2:
                    sp.dma_start(xin[k][:, :], x_p[k * P:(k + 1) * P, :]).then_inc(n1.landed[k], 16)
            sp.dma_start(wdt_raw[:, :].rearrange("p (k n) -> p k n", n=HEADS),
                         win[:, :, COL_DT:COL_DT + HEADS]).then_inc(wdt_in, 16)
            for v in range(2):
                load_unit(v, v, win[:, :, COL_Z + v * P:COL_Z + (v + 1) * P], first=True)
            with sp.Fori(1, 4) as i:
                for v in range(2):
                    sp.wait_ge(n1.turned, i * 2 + v - 1)
                    sp.dma_start(xin[v][:, :], x_p[ds((i * 2 + v) * P, P), :]).then_inc(n1.landed[v], 16)
            sp.wait_ge(n1.turned, 7)
            sp.dma_start(xin[0][0:DEC, :], x_s).then_inc(n1.landed[0], 16)
            with sp.Fori(0, 8) as i:
                for v in range(2):
                    load_unit(i * 2 + v + 2, v, win[:, :, ds((i * 2 + v + 2) * P + COL_Z, P)])
                    sp.wait_ge(ada_used, (i * 2 + v) * 16 + ADA_DVE * 16 - 16)
                    sp.dma_start(ada[v][:, :, :], wada[:, :, ds((i * 2 + v + 8) * 256, 256)]).then_inc(ada_in[v], 16)
            with sp.Fori(0, 11) as i:
                for v in range(2):
                    load_unit(i * 2 + v + 18, v, win[:, :, ds((i * 2 + v + 2) * P + COL_XBC, P)])

            wba, wbb, wo = kmaj(A["w_branch_a"][0]), kmaj(A["w_branch_b"][0]), kmaj(A["w_out"][0])

            def y_out(t, k):
                sp.dma_start(y_c[t].rearrange("f p l -> p f l"), yg[k][:, :, :]).then_inc(y_store[k], 16)

            def chunk_loads(b, first=False):
                for k in range(3):
                    t = b * 3 + k
                    sp.wait_ge(yg_ready, t + 1)
                    if not first:
                        y_out(t - 3, k)
                    sp.dma_start(xs_in[k][:, :, :], xs_c[t].rearrange("f p l -> p f l")).then_inc(chunk_in[k], 16)
                    sp.dma_start(bc_in[k][:, :, :], bc_c.rearrange("b t p l -> t p b l")[t]).then_inc(chunk_in[k], 16)
                    sp.dma_start(z_in[k][:, :, :], z_c[t].rearrange("f p l -> p f l")).then_inc(chunk_in[k], 16)
                    sp.dma_start(acs_in[k][:, :, :], acs_c[t].partition_broadcast(P)).then_inc(chunk_in[k], 16)

            for v in range(2):
                load_unit(U_SSD + v, v, win[:, :, v * P:(v + 1) * P])
            sp.wait_ge(acs_out, 16 * GROUPS)
            for q in range(2):
                sp.wait_ge(z_store[q], 8 * 32)
                sp.wait_ge(cv_store[q], 12 * 32)
            sp.wait_ge(cv_silu, CT)
            chunk_loads(0, first=True)
            for v in range(2):
                load_unit(U_SSD + 2 + v, v, win[:, :, (2 + v) * P:(3 + v) * P])
            with sp.Fori(1, 3) as b:
                chunk_loads(b)
                for v in range(2):
                    load_unit(b * 2 + v + U_SSD + 2, v, win[:, :, ds((b * 2 + v + 2) * P, P)])
            with sp.Fori(3, 11) as b:
                chunk_loads(b)
                for v in range(2):
                    load_unit(b * 2 + v + U_SSD + 2, v, win[:, :, ds((b * 2 + v + 2 - KT) * P + COL_GATES, P)])
            chunk_loads(11)
            load_unit(U_B, 0, wbb[:, 0:4, 0:256])
            for k in range(3):
                sp.wait_ge(yg_ready, 33 + k + 4)
                y_out(33 + k, k)
            for k in range(3):
                sp.wait_ge(y_store[k], 12 * 16)
            load_unit(U_B + 1, 1, wbb[:, 0:4, 256:512])
            sp.wait_ge(edge_t, 12)
            sp.wait_ge(edge_v, 8)
            for q in range(2):
                sp.wait_ge(edge_store[q], 16 * GROUPS)
                sp.wait_ge(gp_store[q], 12 * 16)

            def y_again(g):
                if g >= 2:
                    sp.wait_ge(yb_lo, 4 * (g - 1))
                for f in range(4):
                    sp.dma_start(y_in[g % 2][:, f, 0:SEQ].rearrange("p (c l) -> p c l", l=CH),
                                 y_c[g * NCH:g * NCH + 8, f].rearrange("c p l -> p c l")).then_inc(y_back[g % 2], 16)
                sp.dma_start(y_in[g % 2][:, :, SEQ:T], y_c[g * NCH + 8, :, :, 0:DEC].rearrange("f p l -> p f l"))\
                  .then_inc(y_back[g % 2], 16)

            y_again(0)
            for g in range(GROUPS):
                if g < GROUPS - 1:
                    y_again(g + 1)
                for q in range(4):
                    u = 4 * g + q + 2
                    if u < 16:
                        load_unit(U_B + u, u % 2, wbb[:, 4 * (u // 4):4 * (u // 4) + 4, (u % 4) * 256:(u % 4 + 1) * 256])
            wpg = A["pool_group_w"][0].rearrange("g c d -> (g c) d").rearrange("(q p) n -> p q n", p=P)
            for v in range(2):
                load_unit(U_POOL + v, v, wpg[:, 4 * v:4 * v + 4, :])
            for q in range(2):
                sp.wait_ge(gp_store[q], 12 * 16)
            sp.wait_ge(mm["brb"], 4 * 24)
            for j in range(KT):
                if j >= 2:
                    sp.wait_ge(pm_l, j - 1)
                sp.dma_start(pl_in[j % 2][:, PW:PW + SEQ], gp_s[j][:, 0:SEQ]).then_inc(pl_landed[j % 2], 16)
                sp.dma_start(pl_in[j % 2][:, SEQ + 2 * PW:SEQ + 2 * PW + DEC], gp_s[j][:, SEQ:T])\
                  .then_inc(pl_landed[j % 2], 16)
                if j == 1:
                    for v in range(2):
                        load_unit(U_A + v, v, wba[:, :, v * P:(v + 1) * P])

            def load_gates(m, v):
                sp.wait_ge(mg_vec, m * 5)
                for q in range(2):
                    sp.dma_start(gates[v][q][:, :], gp_s[m + (1 + q) * KT]).then_inc(gate_in[v], 16)

            sp.wait_ge(ab_lo, KT)
            sp.wait_ge(ptail_out, 32)
            with sp.Fori(0, 3) as i:
                for v in range(2):
                    load_gates(i * 2 + v, v)
                    load_unit(i * 2 + v + U_A + 2, v, wba[:, :, ds((i * 2 + v + 2) * P, P)])
            for v in range(2):
                load_gates(6 + v, v)
                load_unit(U_OUT + v, v, wo[:, :, v * P:(v + 1) * P])
            with sp.Fori(0, 3) as i:
                for v in range(2):
                    load_unit(i * 2 + v + U_OUT + 2, v, wo[:, :, ds((i * 2 + v + 2) * P, P)])
            wg, wu, wd = kmaj(A["w_ffn_gate"][0]), kmaj(A["w_ffn_up"][0]), kmaj(A["w_ffn_down"][0])
            load_unit(U_FFN, 0, wg[:, :, 0:P])
            load_unit(U_FFN + 1, 1, wu[:, :, 0:P])
            sp.wait_ge(mm["out"], 24)

            def pairs(body):
                with sp.Fori(0, 4) as i:
                    body([(i * 2, 0, i), (i * 2 + 1, 1, i)], CH)
                body([(8, 0, 4)], DEC)

            def again_x(tiles, L):
                for t, v, i in tiles:
                    sp.wait_ge(n2.added, t + 1)
                    src = x_s if L == DEC else x_p[ds(t * P, P), :]
                    sp.dma_start(xr[v][0:L, :, :], src.rearrange("t (f c) -> t f c", c=P)).then_inc(n2.landed[v], 16)

            pairs(again_x)
            load_unit(U_FFN + 2, 0, wg[:, :, P:2 * P])
            load_unit(U_FFN + 3, 1, wu[:, :, P:2 * P])
            with sp.Fori(1, FG) as i:
                u0 = i * 6 + (U_FFN - 2)
                load_unit(u0, 0, wg[:, :, ds(i * 2 * P, P)])
                load_unit(u0 + 1, 1, wu[:, :, ds(i * 2 * P, P)])
                for v in range(2):
                    load_unit(u0 + 2 + v, v, wd[:, ds(i * 2 - 2, 2), v * 512:(v + 1) * 512])
                load_unit(u0 + 4, 0, wg[:, :, ds(i * 2 * P + P, P)])
                load_unit(u0 + 5, 1, wu[:, :, ds(i * 2 * P + P, P)])
            for v in range(2):
                load_unit(U_END - 2 + v, v, wd[:, 2 * FG - 2:2 * FG, v * 512:(v + 1) * 512])
            sp.wait_ge(mm["ffn"], FFN_SUBS)
            sp.dma_start(final_w[:, :, :], A["final_norm_w"].rearrange("(f c) -> f c", c=P).partition_broadcast(P))\
              .then_inc(fw_in, 16)

            def x2_again(t, v, L=CH):
                sp.wait_ge(n3.added, t + 1)
                sp.dma_start(fr[v][0:L, :, :], x2_s[t][0:L, :].rearrange("t (f c) -> t f c", c=P))\
                  .then_inc(n3.landed[v], 16)

            def y_final(t, v, L=CH):
                sp.wait_ge(n3.scaled, t + 1)
                dst = yo_s if L == DEC else yo_p[ds(t * P, P), :]
                sp.dma_start(dst.rearrange("t (f c) -> t f c", c=P), fo[v][0:L, :, :]).then_inc(out_sem[v], 16)

            for v in range(2):
                x2_again(v, v)
            with sp.Fori(1, 4) as i:
                for v in range(2):
                    x2_again(i * 2 + v, v)
                for v in range(2):
                    y_final(i * 2 + v - 2, v)
            x2_again(8, 0, DEC)
            for v in range(2):
                y_final(6 + v, v)
            y_final(8, 0, DEC)
            for v in range(2):
                sp.wait_ge(out_sem[v], 16 * (5 - v))

        @block.gpsimd
        def _(pool):
            pool.memset(ones[:, :], 1.0).then_inc(consts, 1)
            pool.memset(ident[:, :], 0.0).then_inc(consts, 1)
            pool.memset(half[:, :], -0.5).then_inc(consts, 1)
            for k in range(PW):
                pool.memset(inv_pos[:, k:k + 1], 1.0 / (k + 1)).then_inc(consts, 1)
            pool.memset(dt_in[:, :, :], 0.0).then_inc(consts, 1)
            for v in range(2):
                pool.memset(raw[v][:, 0:3], 0.0).then_inc(consts, 1)
                pool.memset(zb[v][:, T:T + DEC], 0.0).then_inc(consts, 1)
                pool.memset(cv[v][:, T + 3:T + 3 + DEC], 0.0).then_inc(consts, 1)
            pool.wait_ge(consts, N_MEMSET)
            pool.affine_select(out=ident[:, :], in_=ident[:, :], compare_op=ALU.not_equal, fill=1.0, base=0,
                               pattern=[[-1, P]], channel_multiplier=1).then_inc(consts, 1)
            pool.affine_select(out=upper[:, :], in_=ones[:, :], compare_op=ALU.is_ge, fill=0.0, base=0,
                               pattern=[[1, P]], channel_multiplier=-1).then_inc(consts, 1)

            def powers(n, t, v, L=P):
                pool.wait_ge(n.var, t + 1)
                pool.tensor_tensor(small[0:L, 4 + v:5 + v], small[0:L, 2 + v:3 + v], half[0:L, 0:1], ALU.pow)\
                    .then_inc(n.rms, 1)

            with pool.Fori(0, 4) as i:
                for v in range(2):
                    powers(n1, i * 2 + v, v)
            powers(n1, 8, 0, DEC)
            ssm_in = A["state_ssm"][0, 0].rearrange("h p n -> (h p) n").rearrange("(g i q) n -> g q i n", g=GROUPS, q=P)
            ssm_out = [O[k][0, 0].rearrange("h p n -> (h p) n").rearrange("(g i q) n -> g q i n", g=GROUPS, q=P)
                       for k in (4, 7)]
            pool.wait_ge(cv_silu, CT)
            for q in range(2):
                pool.wait_ge(cv_store[q], 12 * 32)

            def causal(g, j, k):
                pool.wait_ge(chunk_in[k], (g * 3 + j) * 64 + 64)
                pool.sem_inc(mask_turn, 1)
                pool.affine_select(out=acs_in[k][:, :, :], in_=acs_in[k][:, :, :], compare_op=ALU.is_ge, fill=-1e30,
                                   base=0, pattern=[[0, HPG], [1, CH]], channel_multiplier=-1).then_inc(masked, 1)

            def store_state(q, g):
                pool.wait_ge(edge_v, g * 2 + q + 1)
                pool.dma_start(ssm_out[q][g], state_out[q][:, :, :]).then_inc(edge_store[q], 16)

            for g in range(GROUPS):
                for k in range(3):
                    causal(g, 0, k)
                if g:
                    store_state(1, g - 1)
                    pool.wait_ge(edge_t, g * 3)
                pool.dma_start(state_in[:, :, :], ssm_in[g]).then_inc(st_in, 16)
                with pool.Fori(1, 3) as j:
                    for k in range(3):
                        causal(g, j, k)
                store_state(0, g)
            store_state(1, GROUPS - 1)
            pool.wait_ge(tails_v, 2)
            for q, k in enumerate((3, 6)):
                pool.dma_start(O[k][0, 0].rearrange("k (t c) -> (k t) c", c=P), tail_rows[:, q, :]).then_inc(tails_out, 16)
            for g in range(GROUPS):
                if g:
                    pool.wait_ge(rms_wide, g)
                pool.wait_ge(rms_vec, 2 * g + 2)
                for r, c in [(P, slice(0, NCH - 1)), (DEC, slice(NCH - 1, NCH))]:
                    w_ = c.stop - c.start
                    pool.tensor_tensor(rms_g[0:r, c], rms_v[0:r, c], half[0:r, 0:1].broadcast_to([r, w_]), ALU.pow)\
                        .then_inc(rms_pow, 1)
            pool.wait_ge(ptail_v, 2)
            for q, k in enumerate((2, 5)):
                pool.dma_start(O[k][0, 0].rearrange("k (t c) -> (k t) c", c=P), pool_rows[:, q, :]).then_inc(ptail_out, 16)
            def pairs(body):
                with pool.Fori(0, 4) as i:
                    body([(i * 2, 0, i), (i * 2 + 1, 1, i)], CH)
                body([(8, 0, 4)], DEC)

            def norm2_tiles(tiles, L):
                for t, v, i in tiles:
                    powers(n2, t, v, L)

            def norm3_tiles(tiles, L):
                for t, v, i in tiles:
                    powers(n3, t, v, L)

            pairs(norm2_tiles)
            pairs(norm3_tiles)
            for sem, n in [(edge_store[0], 4), (edge_store[1], 4), (tails_out, 2), (ptail_out, 2)]:
                pool.wait_ge(sem, 16 * n)

        @block.scalar
        def _(act):
            def hi(u, v, ph, done):
                act.wait_ge(w_in_[v], (u - v) * 8 + 16)
                act.wait_ge(mm[ph], done)
                act.activation(w_split[v][0][:, :], w_raw[v][:, :], ACT.Copy).then_inc(hi_ready, 1)

            act.wait_ge(cols_ready, 4)
            act.activation(silu_c[:, :, :].rearrange("p k s -> p s k"),
                           cols_vec[:, 88:104].rearrange("p (s k) -> p s k", s=2), ACT.Silu).then_inc(c_ready, 1)
            act.wait_ge(rows_in, 16 * N_ROWS)
            act.activation(bc_head[:, 1, :], bc_head[:, 1, :], ACT.Exp).then_inc(c_ready, 1)
            hi(0, 0, "z", 0)
            act.wait_ge(wdt_in, 16)
            act.activation(wdt[0][:, :], wdt_raw[:, :], ACT.Copy).then_inc(wdt_h, 1)

            def squares(n, src, jk, v, t, L=P):
                act.wait_ge(n.squared, t)
                act.activation(jk[0:L], src[0:L], ACT.Square, accum_out=small[0:L, v:v + 1]).then_inc(n.squared, 1)

            def norm1_tiles(tiles, L=P):
                for t, v in tiles:
                    act.wait_ge(n1.landed[v], (t - v) * 8 + 16)
                    squares(n1, xin[v][:, :], junk[:, :], v, t, L)
                for t, v in tiles:
                    act.wait_ge(n1.modulated, t + 3)
                    tok = ds(t * P, L)
                    act.activation(act_a[0][:, :, tok], hf[v][:, :, 0:L], ACT.Copy).then_inc(n1.hi, 1)

            with act.Fori(0, 4) as i:
                norm1_tiles([(i * 2, 0), (i * 2 + 1, 1)])
            norm1_tiles([(8, 0)], DEC)
            for n, (o, w) in enumerate(SUBS):
                act.wait_ge(dt_mm, n + 1)
                act.activation(dt_row[:, o:o + w], PS[0:HEADS, n, 0:w], ACT.Copy).then_inc(dt_copied, 1)
            act.wait_ge(dt_vec, 2)
            act.activation(dt_q[:, :, :], dt_in[:, :, :], ACT.Abs).then_inc(dt_act, 1)
            act.wait_ge(dt_act, 1)
            act.activation(dt_e[:, :, :], dt_q[:, :, :], ACT.Exp, scale=-1.0).then_inc(dt_act, 1)

            act.sem_inc(mm_free["z"], 3)
            zv = z_c.rearrange("(g c) f p l -> g f p c l", g=GROUPS)
            with act.Fori(0, GROUPS) as g:
                with act.Fori(0, 2) as i:
                    for v in range(2):
                        u = g * 4 + i * 2 + v
                        hi(u + 1, 1 - v, "z", u * 3)
                        act.wait_ge(z_store[v], (g * 2 + i) * 32)
                        for n, (o, w) in enumerate(SUBS):
                            act.wait_ge(mm["z"], u * 3 + n + 1)
                            act.activation(zb[v][:, o:o + w], PS[:, n, 0:w], ACT.Silu).then_inc(mm_free["z"], 1)
                        act.wait_ge(mm_free["z"], u * 3 + 6)
                        dst = zv[g][i * 2 + v]
                        act.dma_start(dst[:, 0:NCH - 1, :], zb[v][:, 0:SEQ].rearrange("p (c l) -> p c l", l=CH))\
                           .then_inc(z_store[v], 16)
                        act.dma_start(dst[:, NCH - 1, :], zb[v][:, SEQ:SEQ + CH]).then_inc(z_store[v], 16)
            act.wait_ge(dt_vec, DV_TAB)
            act.activation(eacs_tab[:, :, :], dt_s[:, :, :], ACT.Exp).then_inc(dt_act, 1)
            act.activation(dend_tab[:, :, :], dt_e[:, :, :], ACT.Exp).then_inc(dt_act, 1)
            act.activation(bdec_tab[:, :, :], dt_p[:, :, :], ACT.Exp).then_inc(dt_act, 1)
            for g in range(GROUPS):
                act.dma_start(acs_c[g * NCH:(g + 1) * NCH].rearrange("c h l -> h c l"),
                              acs_row[g * HPG:(g + 1) * HPG, :].rearrange("h (c l) -> h c l", l=CH)).then_inc(acs_out, 16)
            act.sem_inc(mm_free["xbc"], 3)

            def conv_tile(n_, v, dst):
                u = n_ + 16
                hi(u + 1, 1 - v, "xbc", n_ * 3)
                act.wait_ge(cv_step, n_ * 4 + 4)
                for n, (o, w) in enumerate(SUBS):
                    act.wait_ge(mm["xbc"], n_ * 3 + n + 1)
                    if n < 2:
                        act.activation(raw[v][:, 3 + o:3 + o + w], PS[:, n, 0:w], ACT.Copy).then_inc(mm_free["xbc"], 1)
                    else:
                        act.activation(raw[v][:, 3 + o:3 + SEQ], PS[:, n, 0:SEQ - o], ACT.Copy)
                        act.activation(raw[v][:, 6 + SEQ:6 + T], PS[:, n, SEQ - o:w], ACT.Copy).then_inc(mm_free["xbc"], 1)
                act.wait_ge(cv_step, n_ * 4 + 12)
                act.activation(cv[v][:, 0:T + 3], cv[v][:, 0:T + 3], ACT.Silu).then_inc(cv_silu, 1)
                act.wait_ge(cv_silu, n_ + 1)
                act.dma_start(dst[:, 0:NCH - 1, :], cv[v][:, 0:SEQ].rearrange("p (c l) -> p c l", l=CH))\
                   .then_inc(cv_store[v], 16)
                act.dma_start(dst[:, NCH - 1, :], cv[v][:, SEQ + 3:SEQ + 3 + CH]).then_inc(cv_store[v], 16)

            xv = xs_c.rearrange("(g c) f p l -> g f p c l", g=GROUPS)
            bv = bc_c.rearrange("b (g c) p l -> b g p c l", g=GROUPS)
            with act.Fori(0, GROUPS) as g:
                with act.Fori(0, 2) as i:
                    for v in range(2):
                        conv_tile(g * 4 + i * 2 + v, v, xv[g][i * 2 + v])
            with act.Fori(0, 2) as b:
                with act.Fori(0, 2) as i:
                    for v in range(2):
                        conv_tile(b * 4 + i * 2 + v + 16, v, bv[b][i * 2 + v])

            act.sem_inc(mm_free["ssd"], 3)
            act.wait_ge(cv_store[0], 12 * 32)
            act.wait_ge(cv_store[1], 12 * 32)
            act.wait_ge(z_store[0], 8 * 32)
            act.wait_ge(z_store[1], 8 * 32)
            act.wait_ge(acs_out, 16 * GROUPS)

            def decays(g, j, k):
                t = g * NCH + j * 3 + k
                act.wait_ge(masked, t + 1)
                act.wait_ge(v_mix, t)
                for h in range(HPG):
                    e = act.activation(decay[:, h, :], acs_in[k][:, h, :], ACT.Exp,
                                       bias=nacs_tab[:, :, :].rearrange("p c h -> p (c h)")
                                       [:, ds((j * 3 + k) * HEADS + g * HPG + h, 1)])
                e.then_inc(decay_ready, 1)

            def copy_third(b, q):
                v, n = divmod(q, 3)
                o, w = SUBS[n]
                if n == 0:
                    act.wait_ge(gp_store[v], b * 16)
                act.wait_ge(mm["ssd"], b * 6 + q + 1)
                act.activation(gp[v][:, o:o + w], PS[:, n, 0:w], ACT.Copy).then_inc(mm_free["ssd"], 1)
                if n == 2:
                    act.wait_ge(mm_free["ssd"], b * 6 + q + 4)
                    act.dma_start(gp_s[b * 2 + v], gp[v][:, :]).then_inc(gp_store[v], 16)

            def three_chunks(g, j, ahead):
                b = g * 3 + j
                hi(b * 2 + U_SSD + 1, 1, "ssd", b * 6)
                for k in range(3):
                    if k < 2:
                        decays(g, j, k + 1)
                    elif ahead:
                        decays(*ahead)
                    copy_third(b, 2 * k)
                    if k == 1:
                        hi(b * 2 + U_SSD + 2, 0, "ssd", b * 6 + 3)
                    copy_third(b, 2 * k + 1)

            def group(g, last):
                with act.Fori(0, 2) as j:
                    three_chunks(g, j, (g, j + 1, 0))
                three_chunks(g, 2, None if last else (g + 1, 0, 0))

            decays(0, 0, 0)
            with act.Fori(0, GROUPS - 1) as g:
                group(g, False)
            group(GROUPS - 1, True)

            def group_norm(g, piece):
                v = g % 2
                if piece == 0:
                    act.wait_ge(y_back[v], 80 * (g // 2 + 1))
                    if g:
                        act.wait_ge(gs_mm, g)
                    for f in range(4):
                        act.activation(ysq[:, f, :], y_in[v][:, f, :], ACT.Square).then_inc(ysq_ready, 1)
                if piece >= 2:
                    if piece == 2 and g >= 2:
                        act.wait_ge(mm["brb"], 24 * (g - 1))
                    for f in range(2 * piece - 4, 2 * piece - 2):
                        act.wait_ge(yn_ready, 4 * g + f + 1)
                        act.activation(act_a[0][:, 4 * v + f, :], y_in[v][:, f, :], ACT.Copy).then_inc(yb_hi, 1)

            act.wait_ge(mm["ssd"], 72)
            act.wait_ge(edge_v, 8)
            for q in range(2):
                act.wait_ge(edge_store[q], 16 * GROUPS)
                act.wait_ge(gp_store[q], 12 * 16)
            for piece in range(4):
                group_norm(0, piece)
            for g in range(GROUPS):
                for q in range(4):
                    hi(U_B + 4 * g + q + 1, 1 - q % 2, "brb", 6 * (4 * g + q))
                    if g < GROUPS - 1:
                        group_norm(g + 1, q)
            for gi in range(GROUPS):
                if gi == 0:
                    hi(U_POOL + 1, 1, "brb", 96)
                if gi == 2:
                    hi(U_A, 0, "pool", 12)
                for m in range(2):
                    j = 2 * gi + m
                    act.wait_ge(pl_vec, PL_DONE[j])
                    if gi:
                        act.wait_ge(mm["pool"], 6 * gi)
                    act.activation(pm_hi[:, m, :], pool_f[:, :], ACT.Copy).then_inc(pm_h, 1)
                for m in range(2):
                    j = 2 * gi + m
                    act.wait_ge(mm_free["pool"], 3 * j + 6)
                    if j == 0:
                        act.wait_ge(tails_out, 32)
                    act.activation(act_b[0][:, j, :], a_val[m][:, :], ACT.Copy).then_inc(ab_hi, 1)
            act.wait_ge(mm["pool"], 24)
            with act.Fori(0, 4) as i:
                for v in range(2):
                    hi(i * 2 + v + U_A + 1, 1 - v, "bra", i * 6 + 3 * v)
                    act.wait_ge(gate_in[v], i * 32 + 32)
                    for q in range(2):
                        act.activation(gates[v][q][:, :], gates[v][q][:, :], ACT.Tanh, scale=0.5).then_inc(gate_tanh, 1)
            act.wait_ge(mg_vec, 5 * KT + 5)
            for m in range(KT):
                act.activation(act_a[0][:, m, :], acc[:, m, :], ACT.Copy, scale=0.5).then_inc(mg_hi, 1)
            with act.Fori(0, 4) as i:
                for v in range(2):
                    hi(i * 2 + v + U_OUT + 1, 1 - v, "out", i * 6 + 3 * v)

            def pairs(body):
                with act.Fori(0, 4) as i:
                    body([(i * 2, 0, i), (i * 2 + 1, 1, i)], CH, 0)
                body([(8, 0, 4)], DEC, 1)

            def stage(n, dst, gate, t, s_, L):
                act.wait_ge(n.turned_in, t + 1)
                for f in range(KT):
                    e = act.activation(dst[:, f, 0:L], acc[:, f, :][:, ds(t * P, L)], ACT.Copy,
                                       scale=mods[:, gate + f, s_:s_ + 1])
                e.then_inc(n.staged, 1)

            def norm2_tiles(tiles, L, s_):
                for t, v, i in tiles:
                    stage(n2, st[v], GATE1, t, s_, L)
                for t, v, i in tiles:
                    act.wait_ge(n2.added, t + 3)
                    act.dma_start(x2_s[t][0:L, :].rearrange("t (f c) -> t f c", c=P), x2[v][0:L, :, :]).then_inc(x2_out[v], 16)
                    squares(n2, x2[v][:, :, :], g2_junk[:, :, :], v, t, L)
                for t, v, i in tiles:
                    act.wait_ge(n2.modulated, t + 3)
                    act.activation(act_b[0][:, :, ds(t * P, L)], h2[v][:, :, 0:L], ACT.Copy).then_inc(n2.hi, 1)

            act.wait_ge(mm_free["out"], 27)
            pairs(norm2_tiles)

            act.wait_ge(n2.lo, NCH)
            for q in range(2):
                act.wait_ge(x2_out[q], 16 * (5 - q))

            def gate_thirds(i, q, sub0):
                for n, (o, w) in enumerate(SUBS):
                    act.wait_ge(mm["ffn"], sub0 + n + 1)
                    act.activation(silu_g[:, o:o + w], PS[:, n, 0:w], ACT.Silu).then_inc(f_silu, 1)

            def f_part(q, dve_before):
                act.wait_ge(mm_free["ffn"], dve_before + 6)
                act.activation(f_split[0][:, q, :], f_val[:, :], ACT.Copy).then_inc(f_hi, 1)

            hi(U_FFN + 1, 1, "ffn", 0)
            gate_thirds(0, 0, 0)
            hi(U_FFN + 2, 0, "ffn", 3)
            f_part(0, 0)
            hi(U_FFN + 3, 1, "ffn", 6)
            gate_thirds(0, 1, 6)
            hi(U_FFN + 4, 0, "ffn", 9)
            f_part(1, 3)
            with act.Fori(1, FG) as i:
                u0, sub0, dve0 = i * 6 + (U_FFN - 2), i * 36 - 24, i * 30 - 24
                hi(u0 + 1, 1, "ffn", sub0)
                gate_thirds(i, 0, sub0)
                hi(u0 + 2, 0, "ffn", sub0 + 3)
                hi(u0 + 3, 1, "ffn", sub0 + 6)
                hi(u0 + 4, 0, "ffn", sub0 + 18)
                act.wait_ge(mm["ffn"], sub0 + 30)
                f_part(0, dve0)
                hi(u0 + 5, 1, "ffn", sub0 + 30)
                gate_thirds(i, 1, sub0 + 30)
                hi(u0 + 6, 0, "ffn", sub0 + 33)
                f_part(1, dve0 + 27)
            hi(U_END - 1, 1, "ffn", FFN_SUBS - 24)

            def norm3_tiles(tiles, L, s_):
                for t, v, i in tiles:
                    stage(n3, ft[v], GATE2, t, s_, L)
                for t, v, i in tiles:
                    act.wait_ge(n3.added, t + 3)
                    squares(n3, fx[v][:, :, :], fjunk[:, :, :], v, t, L)

            act.wait_ge(mm_free["ffn"], FFN_DVE + 3)
            pairs(norm3_tiles)

        @block.tensor
        def _(pe):
            def thirds(ph, s0, v, steps, out_m=P, last=None):
                for n, (o, w) in enumerate(SUBS):
                    wait_bank(ph, s0, n)
                    for k, (wt, at_) in enumerate(steps):
                        for q, (a, b) in enumerate(PASSES):
                            e = pe.matmul(PS[0:out_m, n, 0:w], wt[a], at_[b][:, o:o + w],
                                          start=(k == 0 and q == 0), stop=(k == len(steps) - 1 and q == 2))
                    e.then_inc(mm[ph], 1)
                return e

            def wait_bank(ph, s0, n):
                pe.wait_ge(mm_free[ph], s0 + n + 1)

            def unit_ready(u):
                pe.wait_ge(lo_ready, u + 1)

            def cols(v, k, n, j=0, width=P):
                return [w_split[v][p][:, k * n + j:k * n + j + width] for p in range(2)]

            def tile_of(acts, k):
                return [acts[p][:, k, :] for p in range(2)]

            def full_unit(ph, u, s0, v, acts):
                unit_ready(u)
                thirds(ph, s0, v, [(cols(v, k, P), tile_of(acts, k)) for k in range(KT)])

            pe.wait_ge(consts, N_MEMSET + 2)
            pe.wait_ge(rows_in, 16 * N_ROWS)
            for q, (r, n) in enumerate([(rows_conv, 5 * CT), (rows_vec, 104), (rows_hist, 3 * CT), (rows_pool, PW * KT)]):
                e = pe.transpose(PS[:, 6, q * P:q * P + n], r[0:n, :], ident[0:n, 0:n])
            e.then_inc(rows_t, 1)

            def whole_slab(k):
                for j in range(2):
                    for q in range(KT):
                        e = pe.matmul(PS[:, 7, k * 4 + 2 * j:k * 4 + 2 * j + 2], ada_first[k][:, q, j * P:(j + 1) * P],
                                      silu_c[:, q, :], start=(q == 0), stop=(q == KT - 1))
                return e

            def summed_slab(k, slot):
                for j in range(2):
                    for s_ in range(2):
                        e = pe.matmul(PS[:, 7, ds(k * 4 + 2 * j + s_, 1)], ada_sum[:, slot, s_, j * P:(j + 1) * P],
                                      ones[:, 0:1], start=True, stop=True)
                e.then_inc(mods_mm, 1)

            pe.wait_ge(c_ready, 1)
            pe.wait_ge(ada_in[1], 16 * (8 - ADA_DVE))
            for k in range(ADA_DVE, 8):
                e = whole_slab(k)
            e.then_inc(mods_mm, 1)
            for k in range(ADA_DVE):
                pe.wait_ge(ada_used, 16 * k + 16)
                summed_slab(k, k)

            def pairs(body):
                with pe.Fori(0, 4) as i:
                    body([(i * 2, 0, i), (i * 2 + 1, 1, i)], CH)
                body([(8, 0, 4)], DEC)

            def turn(n, src, v, t, b, L):
                pe.wait_ge(n.scaled, t + 1)
                pe.wait_ge(n.modulated, t + 1)
                for f in range(KT):
                    e = pe.transpose(banks2(b)[:, f, 0:L], src[0:L, f, :], ident[0:L, 0:L])
                e.then_inc(n.turned, 1)

            def norm1_tiles(tiles, L):
                for t, v, i in tiles:
                    turn(n1, xin[v][:, :].rearrange("p (f c) -> p f c", c=P), v, t, 2 + 2 * v, L)

            pairs(norm1_tiles)
            pe.wait_ge(n1.lo, NCH)
            pe.wait_ge(wdt_l, 1)
            for n, (o, w) in enumerate(SUBS):
                for k in range(KT):
                    for q, (a, b) in enumerate(PASSES):
                        e = pe.matmul(PS[0:HEADS, n, 0:w], wdt[a][:, k * HEADS:(k + 1) * HEADS], act_a[b][:, k, o:o + w],
                                      start=(k == 0 and q == 0), stop=(k == KT - 1 and q == 2))
                e.then_inc(dt_mm, 1)
            pe.wait_ge(dt_copied, 3)
            for c in range(NCH):
                L = CH if c < NCH - 1 else DEC
                e = pe.transpose(PS[0:L, 5, c * HEADS:(c + 1) * HEADS], dt_row[:, c * CH:c * CH + L],
                                 ident[0:HEADS, 0:HEADS])
            e.then_inc(dt_tok, 1)
            with pe.Fori(0, 8) as i:
                for v in range(2):
                    u = i * 2 + v
                    full_unit("z", u, u * 3, v, act_a)
                    pe.wait_ge(ada_used, u * 16 + (ADA_DVE + 1) * 16)
                    summed_slab(u + 8, v)
            pe.wait_ge(dt_vec, DV_DTA)
            dta = dt_q[:, :, :].rearrange("p c h -> p (c h)")
            pe.matmul(PS[:, 5, 0:NCH * HEADS], upper[:, :], dta, start=True, stop=True)
            pe.matmul(PS[:, 6, 0:NCH * HEADS], ones[:, :], dta, start=True, stop=True)
            for c in range(NCH):
                dst = PS[0:HEADS, 3 + c // 4, (c % 4) * CH:(c % 4 + 1) * CH] if c < 8 else PS[0:HEADS, 6, 384:512]
                e = pe.matmul(dst, dt_q[:, c, :], upper[:, :], start=True, stop=True)
            e.then_inc(dt_cum, 1)
            with pe.Fori(0, 12) as i:
                for v in range(2):
                    u = i * 2 + v
                    full_unit("xbc", u + 16, u * 3, v, act_a)

            def ssd_tokens(g, j, k):
                pe.wait_ge(chunk_in[k], (g * 3 + j) * 64 + 64)
                for f in range(4):
                    pe.transpose(PS[:, 3, f * P:(f + 1) * P], xs_in[k][:, f, :], ident[:, :])
                pe.transpose(PS[:, 4, 0:NS], bc_in[k][:, 0, :], ident[:, :])
                pe.matmul(PS[:, 4, P:2 * P], bc_in[k][:, 0, :], bc_in[k][:, 1, :], start=True, stop=True)\
                  .then_inc(ssd_a, 1)

            def ssd_products(g, j, k, c):
                t = g * NCH + j * 3 + k
                pe.wait_ge(yg_ready, t + 3)
                pe.wait_ge(state_ready, g * 11 + (j * 3 + k + 1 if c < 8 else 10))
                pe.matmul(PS[:, 6, :], bc_in[k][:, 1, :], state[:, :, :], start=True, stop=True)
                pe.wait_ge(v_xend, t + 1)
                pe.wait_ge(v_b, t + 1)
                pe.matmul(PS[:, 7, :], b_tok[:, :], x_end[:, :, :], start=True, stop=True)
                pe.wait_ge(v_mix, t + 1)
                for h in range(HPG):
                    e = pe.matmul(PS[:, 5, h * HD:(h + 1) * HD], mix[:, h, :], x_dt[:, h, :], start=True, stop=True)
                e.then_inc(ssd_b, 1)

            def ssd_turn(g, j, k):
                t = g * NCH + j * 3 + k
                pe.wait_ge(y_ready, t + 1)
                for f in range(4):
                    e = pe.transpose(PS[:, 6, f * P:(f + 1) * P], y_tok[:, 2 * f:2 * f + 2, :], ident[:, :])
                e.then_inc(ssd_c, 1)

            def third_of(b, q):
                v, n = divmod(q, 3)
                o, w = SUBS[n]
                if n == 0:
                    unit_ready(b * 2 + v + U_SSD)
                pe.wait_ge(mm_free["ssd"], b * 6 + q + 1)
                for k in range(KT):
                    for p_, (a, c) in enumerate(PASSES):
                        e = pe.matmul(PS[:, n, 0:w], w_split[v][a][:, k * P:(k + 1) * P], act_a[c][:, k, o:o + w],
                                      start=(k == 0 and p_ == 0), stop=(k == KT - 1 and p_ == 2))
                e.then_inc(mm["ssd"], 1)

            def state_turn(g, want):
                pe.wait_ge(state_ready, g * 11 + want)
                for f in range(4):
                    e = pe.transpose(PS[:, 7, f * P:(f + 1) * P], state[:, 2 * f:2 * f + 2, :], ident[:, :])
                e.then_inc(edge_t, 1)

            def ssd_step(g, j, k, c, ahead):
                b = g * 3 + j
                ssd_products(g, j, k, c)
                if ahead:
                    ssd_tokens(*ahead)
                third_of(b, 2 * k)
                ssd_turn(g, j, k)
                if c == NCH - 2:
                    state_turn(g, 9)
                    pe.wait_ge(st_in, g * 16 + 16)
                    for f in range(4):
                        e = pe.transpose(PS[:, 5, f * P:(f + 1) * P], state_in[:, f, :], ident[:, :])
                    e.then_inc(edge_t, 1)
                if c == NCH - 1:
                    state_turn(g, 11)
                third_of(b, 2 * k + 1)

            def group(g, last):
                with pe.Fori(0, 2) as j:
                    for k in range(3):
                        ssd_step(g, j, k, 0, (g, j, k + 1) if k < 2 else (g, j + 1, 0))
                for k in range(3):
                    ssd_step(g, 2, k, 6 + k, (g, 2, k + 1) if k < 2 else None if last else (g + 1, 0, 0))

            ssd_tokens(0, 0, 0)
            with pe.Fori(0, GROUPS - 1) as g:
                group(g, False)
            group(GROUPS - 1, True)
            pe.wait_ge(edge_v, 2 * GROUPS)
            for q in range(2):
                e = pe.transpose(PS[0:3 * CT, 7, q * P:(q + 1) * P], conv_tail[:, q, :, :], ident[:, :])
            e.then_inc(tails_t, 1)

            def group_sum(g):
                pe.wait_ge(ysq_ready, 4 * g + 4)
                if g:
                    pe.wait_ge(rms_vec, 2 * g)
                for c in range(NCH):
                    L = CH if c < NCH - 1 else DEC
                    for f in range(4):
                        e = pe.matmul(PS[0:L, 3, c:c + 1], ysq[:, f, c * CH:c * CH + L], ones[:, 0:1],
                                      start=(f == 0), stop=(f == 3))
                e.then_inc(gs_mm, 1)

            def spread_rms(g):
                pe.wait_ge(rms_pow, 2 * g + 2)
                if g:
                    pe.wait_ge(yn_ready, 4 * g)
                for c in range(NCH):
                    L = CH if c < NCH - 1 else DEC
                    e = pe.matmul(PS[:, 4 + c // 4, (c % 4) * CH:(c % 4) * CH + L],
                                  rms_g[0:L, c:c + 1].broadcast_to([L, P]), ident[0:L, 0:L], start=True, stop=True)
                e.then_inc(rms_wide, 1)

            group_sum(0)
            spread_rms(0)
            for g in range(GROUPS):
                pe.wait_ge(yb_lo, 4 * g + 4)
                for q in range(4):
                    v = q % 2
                    unit_ready(U_B + 4 * g + q)
                    for m in range(2):
                        thirds("brb", 24 * g + 6 * q + 3 * m, v,
                               [(cols(v, k, 256, m * P), tile_of(act_a, 4 * (g % 2) + k)) for k in range(4)])
                    if q == 0 and g < GROUPS - 1:
                        group_sum(g + 1)
                    if q == 1 and g < GROUPS - 1:
                        spread_rms(g + 1)
            for gi in range(GROUPS):
                v = gi // 2
                if gi % 2 == 0:
                    unit_ready(U_POOL + v)
                pe.wait_ge(pm_l, 2 * gi + 2)
                for m in range(2):
                    thirds("pool", 6 * gi + 3 * m, v,
                           [(cols(v, 2 * (gi % 2) + k, 256, m * P), [pm_hi[:, k, :], pm_lo[:, k, :]]) for k in range(2)])
            pe.wait_ge(pl_vec, PL_DONE[-1])
            for q in range(2):
                e = pe.transpose(PS[0:PW * KT, 7, q * P:(q + 1) * P], pool_tail[:, q, :, :], ident[:, :])
            e.then_inc(ptail_t, 1)
            pe.wait_ge(ab_lo, KT)
            with pe.Fori(0, 4) as i:
                for v in range(2):
                    full_unit("bra", i * 2 + v + U_A, (i * 2 + v) * 3, v, act_b)
            pe.wait_ge(mg_lo, KT)
            with pe.Fori(0, 4) as i:
                for v in range(2):
                    full_unit("out", i * 2 + v + U_OUT, (i * 2 + v) * 3, v, act_a)

            def turn_in(n, src, t, b, L):
                pe.wait_ge(n.staged, t + 1)
                pe.wait_ge(n.added, t + 1)
                for f in range(KT):
                    e = pe.transpose(banks2(b)[0:L, f, :], src[:, f, 0:L], ident[:, :])
                e.then_inc(n.turned_in, 1)

            def norm2_tiles(tiles, L):
                for t, v, i in tiles:
                    turn_in(n2, st[v], t, 4 * v, L)
                for t, v, i in tiles:
                    turn(n2, xn[v][:, :, :], v, t, 4 * v + 2, L)

            pairs(norm2_tiles)

            def f_unit(u, v, sub0, wait):
                unit_ready(u)
                for n, (o, w) in enumerate(SUBS):
                    wait(n)
                    for k in range(KT):
                        for q, (a, b) in enumerate(PASSES):
                            e = pe.matmul(PS[:, n, 0:w], w_split[v][a][:, k * P:(k + 1) * P], act_b[b][:, k, o:o + w],
                                          start=(k == 0 and q == 0), stop=(k == KT - 1 and q == 2))
                    e.then_inc(mm["ffn"], 1)

            def gate_up(i, q, u, dve):
                f_unit(u, 0, None, lambda n: pe.wait_ge(mm_free["ffn"], dve + n + 1))
                f_unit(u + 1, 1, None, lambda n: pe.wait_ge(f_silu, (i * 2 + q) * 3 + n + 1))

            def down(u, dve, v):
                unit_ready(u + v)
                for m in range(4):
                    for n, (o, w) in enumerate(SUBS):
                        pe.wait_ge(mm_free["ffn"], dve + 12 * v + 3 * m + n + 1)
                        for k in range(2):
                            for q, (a, b) in enumerate(PASSES):
                                e = pe.matmul(PS[:, n, 0:w], w_split[v][a][:, k * 512 + m * P:k * 512 + (m + 1) * P],
                                              f_split[b][:, k, o:o + w],
                                              start=(k == 0 and q == 0), stop=(k == 1 and q == 2))
                        e.then_inc(mm["ffn"], 1)

            pe.wait_ge(n2.lo, NCH)
            gate_up(0, 0, U_FFN, 0)
            gate_up(0, 1, U_FFN + 2, 3)
            with pe.Fori(1, FG) as i:
                u0, dve0 = i * 6 + (U_FFN - 2), i * 30 - 24
                gate_up(i, 0, u0, dve0)
                pe.wait_ge(f_lo, i * 2)
                for v in range(2):
                    down(u0 + 2, dve0 + 3, v)
                gate_up(i, 1, u0 + 4, dve0 + 27)
            pe.wait_ge(f_lo, 2 * FG)
            for v in range(2):
                down(U_END - 2, FFN_DVE - 24, v)

            def norm3_tiles(tiles, L):
                for t, v, i in tiles:
                    turn_in(n3, ft[v], t, 4 * v, L)

            pairs(norm3_tiles)

        @block.vector
        def _(dve):
            def lo(u, v):
                dve.wait_ge(hi_ready, u + 1)
                dve.tensor_tensor(w_split[v][1][:, :], w_raw[v][:, :], w_split[v][0][:, :].bitcast(F32), ALU.subtract)\
                   .then_inc(lo_ready, 1)

            dve.wait_ge(rows_t, 1)
            for q, (c_, n) in enumerate([(cols_conv, 5 * CT), (cols_vec, 104), (cols_hist, 3 * CT), (cols_pool, PW * KT)]):
                dve.tensor_copy(c_[:, :], PS[:, 6, q * P:q * P + n]).then_inc(cols_ready, 1)
            dve.wait_ge(c_ready, 2)
            dve.tensor_scalar(bc_head[:, 1, :], bc_head[:, 1, :], -1.0, None, ALU.mult).then_inc(cols_ready, 1)

            def mods_part(a, b):
                for s_ in range(2):
                    dve.tensor_tensor(mods[:, a:b, s_], PS[:, 7, 2 * a:2 * b].rearrange("p (t s) -> p t s", s=2)[:, :, s_],
                                      cols_vec[:, a:b], ALU.add).then_inc(mods_ready, 1)

            def gains(ln, scale_at, w_at, count):
                dve.wait_ge(mods_ready, count)
                for s_ in range(2):
                    dve.scalar_tensor_tensor(gain[:, ln, s_, :], mods[:, scale_at:scale_at + KT, s_], 1.0,
                                             cols_vec[:, w_at:w_at + KT], ALU.add, ALU.mult).then_inc(mods_ready, 1)

            def sum_slab(n, slot, src):
                for k in range(KT):
                    for s_ in range(2):
                        dst, c_ = ada_sum[:, slot, s_, :], silu_c[:, k, s_:s_ + 1]
                        if k == 0:
                            dve.tensor_scalar(dst, src[:, k, :], c_, None, ALU.mult).then_inc(ada_used, 1)
                        else:
                            dve.wait_ge(ada_used, n * 16 + 2 * k + s_ - 1)
                            dve.scalar_tensor_tensor(dst, src[:, k, :], c_, dst, ALU.mult, ALU.add).then_inc(ada_used, 1)

            dve.wait_ge(ada_in[0], 16 * ADA_DVE)
            for k in range(ADA_DVE):
                sum_slab(k, k, ada_first[k])
            lo(0, 0)
            dve.wait_ge(wdt_h, 1)
            dve.tensor_tensor(wdt[1][:, :], wdt_raw[:, :], wdt[0][:, :].bitcast(F32), ALU.subtract).then_inc(wdt_l, 1)
            dve.wait_ge(mods_mm, ADA_DVE + 1)
            dve.wait_ge(cols_ready, 5)
            mods_part(0, 2 * KT)
            gains(0, SCALE1, 48, 2)

            def variance(n, t, v, L=P):
                dve.wait_ge(n.squared, t + 1)
                dve.tensor_scalar(small[0:L, 2 + v:3 + v], small[0:L, v:v + 1], 1.0 / D, EPS, ALU.mult, ALU.add)\
                   .then_inc(n.var, 1)

            def modulate(n, ln, shift, dst, t, v, b, s_, L):
                dve.wait_ge(n.turned, t + 1)
                for f in range(KT):
                    e = dve.tensor_scalar(dst[:, f, 0:L], banks2(b)[:, f, 0:L], gain[:, ln, s_, f:f + 1],
                                          mods[:, shift + f, s_:s_ + 1], ALU.mult, ALU.add)
                e.then_inc(n.modulated, 1)

            def low_part(n, src, act_, t, v, L):
                dve.wait_ge(n.hi, t + 1)
                tok = ds(t * P, L)
                dve.tensor_tensor(act_[1][:, :, tok], src[:, :, 0:L], act_[0][:, :, tok].bitcast(F32), ALU.subtract)\
                   .then_inc(n.lo, 1)

            def pairs(body):
                with dve.Fori(0, 4) as i:
                    body([(i * 2, 0, i), (i * 2 + 1, 1, i)], CH, 0)
                body([(8, 0, 4)], DEC, 1)

            def norm1_tiles(tiles, L, s_):
                for t, v, i in tiles:
                    variance(n1, t, v, L)
                for t, v, i in tiles:
                    dve.wait_ge(n1.rms, t + 1)
                    dve.tensor_scalar(xin[v][0:L, :], xin[v][0:L, :], small[0:L, 4 + v:5 + v], None, ALU.mult)\
                       .then_inc(n1.scaled, 1)
                for t, v, i in tiles:
                    modulate(n1, 0, SHIFT1, hf[v], t, v, 2 + 2 * v, s_, L)
                for t, v, i in tiles:
                    low_part(n1, hf[v], act_a, t, v, L)

            dve.sem_inc(n1.modulated, 2)
            dve.wait_ge(mods_ready, 4)
            pairs(norm1_tiles)

            steps = [0]

            def chain(e):
                steps[0] += 1
                e.then_inc(dt_vec, 1)
                dve.wait_ge(dt_vec, steps[0])

            dve.wait_ge(dt_tok, 1)
            dve.wait_ge(consts, N_MEMSET)
            bias = bc_head[:, 0, :]
            chain(dve.tensor_tensor(dt_in[:, 0:8, :], PS[:, 5, 0:8 * HEADS].rearrange("p (c h) -> p c h", h=HEADS),
                                    bias.unsqueeze(1).broadcast_to([P, 8, HEADS]), ALU.add))
            chain(dve.tensor_tensor(dt_in[0:DEC, 8, :], PS[0:DEC, 5, 8 * HEADS:9 * HEADS], bc_head[0:DEC, 0, :], ALU.add))
            dve.wait_ge(dt_act, 2)
            chain(dve.tensor_scalar(dt_s[:, :, :], dt_e[:, :, :], 2.0, None, ALU.add))
            chain(dve.reciprocal(dt_q[:, :, :], dt_s[:, :, :]))
            chain(dve.tensor_tensor(dt_s[:, :, :], dt_e[:, :, :], dt_q[:, :, :], ALU.mult))
            chain(dve.tensor_tensor(dt_q[:, :, :], dt_s[:, :, :], dt_s[:, :, :], ALU.mult))
            chain(dve.tensor_scalar(dt_p[:, :, :], dt_q[:, :, :], POLY[8], None, ALU.mult))
            for k in range(7, 0, -1):
                chain(dve.scalar_tensor_tensor(dt_p[:, :, :], dt_p[:, :, :], POLY[k], dt_q[:, :, :], ALU.add, ALU.mult))
            chain(dve.scalar_tensor_tensor(dt_p[:, :, :], dt_p[:, :, :], 1.0, dt_s[:, :, :], ALU.add, ALU.mult))
            chain(dve.tensor_scalar(dt_in[:, :, :], dt_in[:, :, :], 0.0, None, ALU.max))
            chain(dve.scalar_tensor_tensor(dt_tab[:, :, :], dt_p[:, :, :], 2.0, dt_in[:, :, :], ALU.mult, ALU.add))
            chain(dve.memset(dt_tab[DEC:P, 8, :], 0.0))
            chain(dve.tensor_tensor(dt_q[:, :, :], dt_tab[:, :, :], bc_head[:, 1, :].unsqueeze(1)
                                    .broadcast_to([P, NCH, HEADS]), ALU.mult))
            assert steps[0] == DV_DTA
            with dve.Fori(0, 8) as i:
                for v in range(2):
                    u = i * 2 + v
                    lo(u + 1, 1 - v)
                    dve.wait_ge(ada_in[v], i * 16 + 16 * (ADA_DVE + 1 if v == 0 else 9 - ADA_DVE))
                    dve.wait_ge(mods_mm, u + ADA_DVE - 1)
                    sum_slab(u + ADA_DVE, v, ada[v])
            dve.wait_ge(dt_cum, 1)
            ps5 = PS[:, 5, 0:NCH * HEADS].rearrange("p (c h) -> p c h", h=HEADS)
            ps6 = PS[:, 6, 0:NCH * HEADS].rearrange("p (c h) -> p c h", h=HEADS)
            chain(dve.tensor_copy(dt_s[:, :, :], ps5))
            chain(dve.tensor_copy(dt_p[:, :, :], ps6))
            chain(dve.tensor_scalar(nacs_tab[:, :, :], dt_s[:, :, :], -1.0, None, ALU.mult))
            chain(dve.tensor_tensor(dt_e[:, :, :], dt_p[:, :, :], dt_s[:, :, :], ALU.subtract))
            chain(dve.tensor_copy(acs_row[:, 0:1024].rearrange("h (b l) -> h b l", b=2), PS[0:HEADS, 3:5, :]))
            chain(dve.tensor_copy(acs_row[:, 1024:1152], PS[0:HEADS, 6, 384:512]))
            assert steps[0] == DV_TAB - 1
            chain(dve.memset(small[:, 6:8], 0.0))
            dve.wait_ge(mods_mm, ADA_DVE + 17)
            mods_part(2 * KT, 48)
            gains(1, SCALE2, 56, 6)

            dve.sem_inc(cv_step, 8)
            with dve.Fori(0, 12) as i:
                for v in range(2):
                    n_ = i * 2 + v
                    lo(n_ + 17, 1 - v)
                    hist = cols_hist[:, :].rearrange("p (k t) -> p k t", k=3)
                    dve.wait_ge(cv_step, n_ * 4 + 4)
                    dve.tensor_copy(raw[v][:, 3 + SEQ:6 + SEQ], hist[:, :, ds(n_, 1)].rearrange("p k o -> p (k o)"))\
                       .then_inc(raw_hist, 1)
                    dve.wait_ge(raw_hist, n_ + 1)
                    dve.wait_ge(mm_free["xbc"], n_ * 3 + 6)
                    dve.tensor_copy(conv_tail[:, :, :, ds(n_, 1)].rearrange("p s k o -> p s (k o)"),
                                    raw[v][:, SEQ:SEQ + 2 * (DEC + 3)].rearrange("p (s k) -> p s k", s=2)[:, :, 0:3])
                    dve.wait_ge(cv_store[v], i * 32)
                    for k in range(4):
                        tap = cols_conv[:, ds(n_ + k * CT, 1)]
                        if k:
                            dve.wait_ge(cv_step, n_ * 4 + k + 8)
                            dve.scalar_tensor_tensor(cv[v][:, 0:T + 3], raw[v][:, k:k + T + 3], tap, cv[v][:, 0:T + 3],
                                                     ALU.mult, ALU.add).then_inc(cv_step, 1)
                        else:
                            dve.tensor_scalar(cv[v][:, 0:T + 3], raw[v][:, 0:T + 3], tap,
                                              cols_conv[:, ds(n_ + 4 * CT, 1)], ALU.mult, ALU.add).then_inc(cv_step, 1)

            def tokens_of(ap):
                return ap.rearrange("p (h d) -> p h d", d=HD)

            def head_col(tab, g, j, k):
                t_ = tab[:, :, :].rearrange("p c h -> p (c h)")
                return t_[:, ds((j * 3 + k) * HEADS + g * HPG, HPG)].unsqueeze(2).broadcast_to([P, HPG, HD])

            def chunk_operands(g, j, k):
                t = g * NCH + j * 3 + k
                dve.wait_ge(ssd_a, t + 1)
                dve.tensor_tensor(x_dt[:, :, :], tokens_of(bank(3)), head_col(dt_tab, g, j, k), ALU.mult).then_inc(v_x, 1)
                dve.tensor_copy(b_tok[:, :], PS[:, 4, 0:NS]).then_inc(v_b, 1)
                dve.tensor_tensor(skip[:, :, :], tokens_of(bank(3)),
                                  bc_head[:, 2, :][:, ds(g * HPG, HPG)].unsqueeze(2).broadcast_to([P, HPG, HD]), ALU.mult)\
                   .then_inc(v_skip, 1)
                dve.wait_ge(v_x, t + 1)
                dve.tensor_tensor(x_end[:, :, :], x_dt[:, :, :], head_col(dend_tab, g, j, k), ALU.mult).then_inc(v_xend, 1)
                dve.wait_ge(decay_ready, t + 1)
                dve.tensor_tensor(mix[:, :, :], decay[:, :, :], PS[:, 4, P:2 * P].unsqueeze(1).broadcast_to([P, HPG, CH]),
                                  ALU.mult).then_inc(v_mix, 1)

            def ssd_step(g, j, k, c, ahead):
                t = g * NCH + j * 3 + k
                dve.wait_ge(ssd_b, t + 1)
                dve.tensor_tensor(y_tok[:, :, :], tokens_of(bank(6)), head_col(eacs_tab, g, j, k), ALU.mult).then_inc(v_y0, 1)
                dve.wait_ge(v_y0, t + 1)
                dve.tensor_tensor(y_tok[:, :, :], tokens_of(bank(5)), y_tok[:, :, :], ALU.add).then_inc(v_y1, 1)
                dve.wait_ge(v_y1, t + 1)
                dve.wait_ge(v_skip, t + 1)
                dve.tensor_tensor(y_tok[:, :, :], y_tok[:, :, :], skip[:, :, :], ALU.add).then_inc(y_ready, 1)
                dve.wait_ge(state_ready, g * 11 + (j * 3 + k + 1 if c < 8 else 10))
                dve.tensor_tensor(state[:, :, :], state[:, :, :], head_col(bdec_tab, g, j, k), ALU.mult).then_inc(v_s0, 1)
                dve.wait_ge(v_s0, t + 1)
                dve.tensor_tensor(state[:, :, :], tokens_of(bank(7)), state[:, :, :], ALU.add).then_inc(state_ready, 1)
                if ahead:
                    chunk_operands(*ahead)
                dve.wait_ge(y_store[k], (g * 3 + j) * 16)
                dve.wait_ge(ssd_c, t + 1)
                dve.tensor_tensor(yg[k][:, :, :], bank(6).rearrange("p (f l) -> p f l", f=4), z_in[k][:, :, :], ALU.mult)\
                   .then_inc(yg_ready, 1)
                if c == NCH - 2:
                    dve.wait_ge(edge_t, g * 3 + 1)
                    dve.wait_ge(edge_store[0], g * 16)
                    dve.tensor_copy(state_out[0][:, :, :], bank(7).rearrange("p (f n) -> p f n", f=4)).then_inc(edge_v, 1)
                    dve.wait_ge(edge_t, g * 3 + 2)
                    dve.tensor_copy(state[:, :, :], tokens_of(bank(5))).then_inc(state_ready, 1)
                if c == NCH - 1:
                    dve.wait_ge(edge_t, g * 3 + 3)
                    dve.wait_ge(edge_store[1], g * 16)
                    dve.tensor_copy(state_out[1][:, :, :], bank(7).rearrange("p (f n) -> p f n", f=4)).then_inc(edge_v, 1)
                    if ahead:
                        dve.memset(state[:, :, :], 0.0).then_inc(state_ready, 1)

            def group(g, last):
                with dve.Fori(0, 2) as j:
                    lo((g * 3 + j) * 2 + U_SSD + 1, 1)
                    for k in range(3):
                        ssd_step(g, j, k, 0, (g, j, k + 1) if k < 2 else (g, j + 1, 0))
                        if k == 1:
                            lo((g * 3 + j) * 2 + U_SSD + 2, 0)
                lo((g * 3 + 2) * 2 + U_SSD + 1, 1)
                for k in range(3):
                    ssd_step(g, 2, k, 6 + k, (g, 2, k + 1) if k < 2 else None if last else (g + 1, 0, 0))
                    if k == 1:
                        lo((g * 3 + 2) * 2 + U_SSD + 2, 0)

            dve.sem_inc(yg_ready, 3)
            dve.wait_ge(dt_act, 5)
            dve.wait_ge(cv_silu, CT)
            for q in range(2):
                dve.wait_ge(cv_store[q], 12 * 32)
                dve.wait_ge(z_store[q], 8 * 32)
            dve.wait_ge(acs_out, 16 * GROUPS)
            dve.memset(state[:, :, :], 0.0).then_inc(state_ready, 1)
            chunk_operands(0, 0, 0)
            with dve.Fori(0, GROUPS - 1) as g:
                group(g, False)
            group(GROUPS - 1, True)

            def group_variance(g):
                if g:
                    dve.wait_ge(rms_pow, 2 * g)
                dve.wait_ge(gs_mm, g + 1)
                for r, c in [(P, slice(0, NCH - 1)), (DEC, slice(NCH - 1, NCH))]:
                    dve.tensor_scalar(rms_v[0:r, c], PS[0:r, 3, c], 1.0 / 512, EPS, ALU.mult, ALU.add).then_inc(rms_vec, 1)

            def y_norm(g, f):
                v = g % 2
                dve.wait_ge(rms_wide, g + 1)
                dve.scalar_tensor_tensor(y_in[v][:, f, :], y_in[v][:, f, :], cols_vec[:, 72 + 4 * g + f:73 + 4 * g + f],
                                         PS[:, 4:7, :].rearrange("p b l -> p (b l)")[:, 0:T], ALU.mult, ALU.mult)\
                   .then_inc(yn_ready, 1)

            def y_low(g, f):
                v = g % 2
                dve.wait_ge(yb_hi, 4 * g + f + 1)
                dve.tensor_tensor(act_a[1][:, 4 * v + f, :], y_in[v][:, f, :],
                                  act_a[0][:, 4 * v + f, :].bitcast(F32), ALU.subtract).then_inc(yb_lo, 1)

            for q in range(2):
                dve.wait_ge(edge_store[q], 16 * GROUPS)
                dve.wait_ge(gp_store[q], 12 * 16)
            for k in range(3):
                dve.wait_ge(y_store[k], 12 * 16)
            dve.wait_ge(tails_t, 1)
            dve.tensor_copy(tail_rows[:, :, :], PS[0:3 * CT, 7, 0:2 * P].rearrange("p (q c) -> p q c", q=2))\
               .then_inc(tails_v, 2)
            dve.sem_inc(mm_free["brb"], 3)
            group_variance(0)
            for f in range(4):
                y_norm(0, f)
                y_low(0, f)
            for g in range(GROUPS):
                for q in range(4):
                    lo(U_B + 4 * g + q + 1, 1 - q % 2)
                    for m in range(2):
                        s0 = 24 * g + 6 * q + 3 * m
                        for n, (o, w) in enumerate(SUBS):
                            dve.wait_ge(mm["brb"], s0 + n + 1)
                            dst = acc[:, 2 * q + m, o:o + w]
                            if g == 0:
                                dve.tensor_copy(dst, PS[:, n, 0:w]).then_inc(mm_free["brb"], 1)
                            else:
                                dve.wait_ge(mm_free["brb"], s0 + n - 20)
                                dve.tensor_tensor(dst, PS[:, n, 0:w], dst, ALU.add).then_inc(mm_free["brb"], 1)
                        piece = 2 * q + m
                        if g < GROUPS - 1 and piece == 2:
                            group_variance(g + 1)
                        if g < GROUPS - 1 and piece >= 4:
                            y_norm(g + 1, piece - 4)
                            if piece > 4:
                                y_low(g + 1, piece - 5)
                if g < GROUPS - 1:
                    y_low(g + 1, 3)

            at_p, at_s = PW, SEQ + 2 * PW
            full = at_s + DEC
            dve.wait_ge(mm["brb"], 96)
            for v in range(2):
                dve.memset(pl_in[v][:, 0:PW], 0.0).then_inc(pl_set, 1)
            dve.sem_inc(mm_free["pool"], 3)
            count = [0]

            def pstep(e):
                count[0] += 1
                e.then_inc(pl_vec, 1)
                dve.wait_ge(pl_vec, count[0])

            for gi in range(GROUPS):
                if gi == 0:
                    lo(U_POOL + 1, 1)
                if gi == 2:
                    lo(U_A, 0)
                wlog = gi + 1
                for m in range(2):
                    j = 2 * gi + m
                    x = pl_in[m]
                    dve.wait_ge(pl_landed[m], 32 * (gi + 1))
                    dve.wait_ge(pl_set, 2)
                    pstep(dve.tensor_copy(x[:, at_s - PW:at_s], cols_pool[:, :].rearrange("p (r t) -> p r t", t=KT)[:, :, j]))
                    pstep(dve.tensor_copy(pool_tail[:, 0, :, j], x[:, at_p + SEQ - PW:at_p + SEQ]))
                    pstep(dve.tensor_copy(pool_tail[:, 1, :, j], x[:, full - PW:full]))
                    cur, first = x, 0
                    for k in range(wlog):
                        nxt, first = [pl_s0, pl_s1][k % 2], first + (1 << k)
                        pstep(dve.tensor_tensor(nxt[:, first:full], cur[:, first:full], cur[:, first - (1 << k):full - (1 << k)],
                                                ALU.add))
                        cur = nxt
                    w_ = 1 << wlog
                    pstep(dve.scalar_tensor_tensor(pool_f[:, 0:SEQ], cur[:, at_p:at_p + SEQ], 1.0 / w_, x[:, at_p:at_p + SEQ],
                                                   ALU.mult, ALU.subtract))
                    pstep(dve.scalar_tensor_tensor(pool_f[:, SEQ:T], cur[:, at_s:full], 1.0 / w_, x[:, at_s:full],
                                                   ALU.mult, ALU.subtract))
                    pstep(dve.tensor_tensor(pool_f[:, 0:w_ - 1], cur[:, at_p:at_p + w_ - 1], inv_pos[:, 0:w_ - 1], ALU.mult))
                    pstep(dve.tensor_tensor(pool_f[:, 0:w_ - 1], pool_f[:, 0:w_ - 1], x[:, at_p:at_p + w_ - 1], ALU.subtract))
                    assert count[0] == PL_DONE[j]
                    dve.wait_ge(pm_h, j + 1)
                    dve.tensor_tensor(pm_lo[:, m, :], pool_f[:, :], pm_hi[:, m, :].bitcast(F32), ALU.subtract).then_inc(pm_l, 1)
                for m in range(2):
                    j = 2 * gi + m
                    for n, (o, w) in enumerate(SUBS):
                        dve.wait_ge(mm["pool"], 3 * j + n + 1)
                        dve.tensor_scalar(a_val[m][:, o:o + w], PS[:, n, 0:w], cols_vec[:, 64 + j:65 + j], None, ALU.mult)\
                           .then_inc(mm_free["pool"], 1)
                for m in range(2):
                    j = 2 * gi + m
                    dve.wait_ge(ab_hi, j + 1)
                    dve.tensor_tensor(act_b[1][:, j, :], a_val[m][:, :], act_b[0][:, j, :].bitcast(F32), ALU.subtract)\
                       .then_inc(ab_lo, 1)
            dve.wait_ge(ptail_t, 1)
            dve.tensor_copy(pool_rows[:, :, :], PS[0:PW * KT, 7, 0:2 * P].rearrange("p (q c) -> p q c", q=2))\
               .then_inc(ptail_v, 2)

            dve.sem_inc(mm_free["bra"], 3)
            dve.sem_inc(mg_vec, 5)
            dve.wait_ge(ptail_out, 32)
            with dve.Fori(0, 4) as i:
                for v in range(2):
                    m = i * 2 + v
                    lo(m + U_A + 1, 1 - v)
                    dve.wait_ge(gate_tanh, m * 2 + 2)
                    dve.wait_ge(mg_vec, m * 5 + 5)
                    for n, (o, w) in enumerate(SUBS):
                        dve.wait_ge(mm["bra"], m * 3 + n + 1)
                        dve.scalar_tensor_tensor(mg_t[:, o:o + w], gates[v][0][:, o:o + w], 1.0, PS[:, n, 0:w],
                                                 ALU.add, ALU.mult).then_inc(mm_free["bra"], 1)
                    row = acc[:, ds(m, 1), :].rearrange("p o t -> p (o t)")
                    dve.scalar_tensor_tensor(gates[v][1][:, :], gates[v][1][:, :], 1.0, row, ALU.add, ALU.mult)\
                       .then_inc(mg_vec, 4)
                    dve.wait_ge(mg_vec, m * 5 + 9)
                    dve.wait_ge(mm_free["bra"], m * 3 + 6)
                    dve.tensor_tensor(row, mg_t[:, :], gates[v][1][:, :], ALU.add).then_inc(mg_vec, 1)
            for m in range(KT):
                dve.wait_ge(mg_hi, m + 1)
                dve.scalar_tensor_tensor(act_a[1][:, m, :], acc[:, m, :], 0.5, act_a[0][:, m, :].bitcast(F32),
                                         ALU.mult, ALU.subtract).then_inc(mg_lo, 1)
            dve.sem_inc(mm_free["out"], 3)
            with dve.Fori(0, 4) as i:
                for v in range(2):
                    m = i * 2 + v
                    lo(m + U_OUT + 1, 1 - v)
                    row = acc[:, ds(m, 1), :].rearrange("p o t -> p (o t)")
                    for n, (o, w) in enumerate(SUBS):
                        dve.wait_ge(mm["out"], m * 3 + n + 1)
                        dve.tensor_copy(row[:, o:o + w], PS[:, n, 0:w]).then_inc(mm_free["out"], 1)

            def norm2_tiles(tiles, L, s_):
                for t, v, i in tiles:
                    dve.wait_ge(n2.landed[v], i * 16 + 16)
                    dve.wait_ge(n2.turned_in, t + 3)
                    dve.wait_ge(x2_out[v], i * 16)
                    dve.tensor_tensor(x2[v][0:L, :, :], banks2(4 * v)[0:L, :, :], xr[v][0:L, :, :], ALU.add).then_inc(n2.added, 1)
                for t, v, i in tiles:
                    variance(n2, t, v, L)
                for t, v, i in tiles:
                    dve.wait_ge(n2.rms, t + 1)
                    dve.tensor_scalar(xn[v][0:L, :, :], x2[v][0:L, :, :], small[0:L, 4 + v:5 + v], None, ALU.mult)\
                       .then_inc(n2.scaled, 1)
                for t, v, i in tiles:
                    modulate(n2, 1, SHIFT2, h2[v], t, v, 4 * v + 2, s_, L)
                for t, v, i in tiles:
                    low_part(n2, h2[v], act_b, t, v, L)

            dve.sem_inc(n2.turned_in, 2)
            dve.sem_inc(n2.added, 2)
            dve.sem_inc(n2.modulated, 2)
            dve.wait_ge(mm["out"], 24)
            pairs(norm2_tiles)

            dve.sem_inc(mm_free["ffn"], 3)
            dve.wait_ge(n2.staged, NCH)
            dve.memset(acc[:, :, :], 0.0).then_inc(y_add, 1)
            for q in range(2):
                dve.wait_ge(x2_out[q], 16 * (5 - q))
            dve.wait_ge(y_add, 1)

            def product(i, q, sub0):
                dve.wait_ge(f_lo, i * 2 + q)
                for n, (o, w) in enumerate(SUBS):
                    dve.wait_ge(f_silu, (i * 2 + q) * 3 + n + 1)
                    dve.wait_ge(mm["ffn"], sub0 + n + 1)
                    dve.tensor_tensor(f_val[:, o:o + w], PS[:, n, 0:w], silu_g[:, o:o + w], ALU.mult)\
                       .then_inc(mm_free["ffn"], 1)

            def f_low(i, q):
                dve.wait_ge(f_hi, i * 2 + q + 1)
                dve.tensor_tensor(f_split[1][:, q, :], f_val[:, :], f_split[0][:, q, :].bitcast(F32), ALU.subtract)\
                   .then_inc(f_lo, 1)

            def sums(v, sub0, dve0):
                for m in range(4):
                    for n, (o, w) in enumerate(SUBS):
                        s_ = 3 * m + n
                        dve.wait_ge(mm["ffn"], sub0 + s_ + 1)
                        dst = acc[:, 4 * v + m, o:o + w]
                        dve.tensor_tensor(dst, PS[:, n, 0:w], dst, ALU.add).then_inc(mm_free["ffn"], 1)

            lo(U_FFN + 1, 1)
            lo(U_FFN + 2, 0)
            product(0, 0, 3)
            lo(U_FFN + 3, 1)
            f_low(0, 0)
            lo(U_FFN + 4, 0)
            product(0, 1, 9)
            with dve.Fori(1, FG) as i:
                u0, sub0, dve0 = i * 6 + (U_FFN - 2), i * 36 - 24, i * 30 - 24
                f_low(i - 1, 1)
                lo(u0 + 1, 1)
                lo(u0 + 2, 0)
                product(i, 0, sub0 + 3)
                lo(u0 + 3, 1)
                dve.wait_ge(mm_free["ffn"], dve0)
                sums(0, sub0 + 6, dve0 + 3)
                lo(u0 + 4, 0)
                sums(1, sub0 + 18, dve0 + 15)
                lo(u0 + 5, 1)
                f_low(i, 0)
                lo(u0 + 6, 0)
                product(i, 1, sub0 + 33)
            f_low(FG - 1, 1)
            lo(U_END - 1, 1)
            dve.wait_ge(mm_free["ffn"], FFN_DVE - 24)
            for v in range(2):
                sums(v, FFN_SUBS - 24 + 12 * v, FFN_DVE - 24 + 12 * v)

            def norm3_tiles(tiles, L, s_):
                for t, v, i in tiles:
                    dve.wait_ge(n3.landed[v], i * 16 + 16)
                    dve.wait_ge(n3.turned_in, t + 3)
                    dve.wait_ge(n3.scaled, i * 2)
                    dve.tensor_tensor(fx[v][0:L, :, :], banks2(4 * v)[0:L, :, :], fr[v][0:L, :, :], ALU.add).then_inc(n3.added, 1)
                for t, v, i in tiles:
                    variance(n3, t, v, L)
                for t, v, i in tiles:
                    dve.wait_ge(n3.rms, t + 1)
                    dve.wait_ge(out_sem[v], i * 16)
                    dve.scalar_tensor_tensor(fo[v][0:L, :, :], fx[v][0:L, :, :], small[0:L, 4 + v:5 + v],
                                             final_w[0:L, :, :], ALU.mult, ALU.mult).then_inc(n3.scaled, 1)

            dve.sem_inc(n3.turned_in, 2)
            dve.sem_inc(n3.added, 2)
            dve.wait_ge(fw_in, 16)
            pairs(norm3_tiles)


_INS = ["x_prompt", "x_sample", "c_prompt", "c_sample", "state_pool", "state_conv", "state_ssm", "w_ada", "b_ada",
        "norm1_w", "norm2_w", "w_in", "pool_group_w", "pool_scale", "conv_w", "conv_b", "dt_bias", "a_log", "d_skip",
        "ssm_norm_w", "w_branch_a", "w_branch_b", "w_out", "w_ffn_gate", "w_ffn_up", "w_ffn_down", "final_norm_w"]
_OUTS = [(1, SEQ, D), (1, DEC, D), (1, 1, PW, D), (1, 1, 3, CONV), (1, 1, HEADS, HD, NS),
         (1, 1, PW, D), (1, 1, 3, CONV), (1, 1, HEADS, HD, NS)]


def kernel(**inputs):
    import numpy as np
    import concourse.bacc as bacc
    from concourse.bass_utils import run_bass_kernel_spmd

    nc = bacc.Bacc("TRN2", target_bir_lowering=False, num_devices=1)
    arrays, ins, outs = {}, {}, []
    for name in _INS:
        a = np.ascontiguousarray(inputs[name])
        arrays[f"in_{name}"] = a
        ins[name] = nc.dram_tensor(f"in_{name}", a.shape, mybir.dt.from_np(a.dtype), kind="ExternalInput").ap()
    for i, shape in enumerate(_OUTS):
        outs.append(nc.dram_tensor(f"out_{i}", shape, F32, kind="ExternalOutput").ap())
    build(nc, ins, outs)
    r = run_bass_kernel_spmd(nc, [arrays], core_ids=[0])
    return tuple(r.results[0][f"out_{i}"] for i in range(len(_OUTS)))
```

```python
import concourse.bass as bass
from concourse import mybir

F32 = mybir.dt.float32
F32R = mybir.dt.float32r
ALU = mybir.AluOpType
ACT = mybir.ActivationFunctionType
ds = bass.ds

P = 128
D = 1024
KT = D // P
SEQ, DEC = 1024, 64
T = SEQ + DEC
CH = 128
NCH = SEQ // CH + 1
HEADS, GROUPS, HPG, HD, NS = 32, 4, 8, 64, 128
DIN = 2 * D
CONV = DIN + 2 * GROUPS * NS
CT = CONV // P
PW = 15
DFF = 2816
FG = DFF // P // 2
EPS = 1e-6
COL_Z, COL_XBC, COL_DT, COL_GATES = D, D + DIN, D + DIN + CONV, D + DIN + CONV + HEADS
THIRD = 364
SUBS = [(0, THIRD), (THIRD, THIRD), (2 * THIRD, T - 2 * THIRD)]
SHIFT1, SCALE1, GATE1, SHIFT2, SCALE2, GATE2 = [i * KT for i in range(6)]
PASSES = [(0, 0), (0, 1), (1, 0)]


def build(nc, A, O):
    base = 16512
    plan = {}

    def at(name, shape, dt, offset):
        n = 1
        for s in shape[1:]:
            n *= s
        plan[name] = (offset, offset + 4 * n)
        return nc.alloc_sbuf_tensor_at(name, shape, dt, offset=offset)

    cursor = [base]
    ADA_SUMMED, ADA_WHOLE = [0, 2, 4, 6, 7], [1, 3, 5]
    ADA_DVE = len(ADA_SUMMED)

    def keep(name, shape, dt=F32):
        t = at(name, shape, dt, cursor[0])
        cursor[0] = (plan[name][1] + 31) // 32 * 32
        return t

    ident = keep("ident", [P, P])
    upper = keep("upper", [P, P])
    ones = keep("ones", [P, P])
    cols_conv = keep("cols_conv", [P, 5 * CT])
    cols_vec = keep("cols_vec", [P, 104])
    cols_hist = keep("cols_hist", [P, 3 * CT])
    cols_pool = keep("cols_pool", [P, PW * KT])
    silu_c = keep("silu_c", [P, KT, 2])
    mods = keep("mods", [P, 48, 2])
    gain = keep("gain", [P, 2, 2, KT])
    bc_head = keep("bc_head", [P, 3, HEADS])
    half = keep("half", [P, 2])
    inv_pos = keep("inv_pos", [P, PW])
    small = keep("small", [P, 8])
    conv_tail = keep("conv_tail", [P, 2, 3, CT])
    dt_tab = keep("dt_tab", [P, NCH, HEADS])
    nacs_tab = keep("nacs_tab", [P, NCH, HEADS])
    eacs_tab = keep("eacs_tab", [P, NCH, HEADS])
    dend_tab = keep("dend_tab", [P, NCH, HEADS])
    bdec_tab = keep("bdec_tab", [P, NCH, HEADS])
    pool_tail = keep("pool_tail", [P, 2, PW, KT])
    pool_rows = keep("pool_rows", [PW * KT, 2, P])
    w_raw = [keep(f"w_raw{i}", [P, 1024]) for i in range(2)]
    w_split = [[keep(f"w_{n}{i}", [P, 1024], F32R) for n in ("hi", "lo")] for i in range(2)]
    RA = cursor[0]
    RB = RA + 2 * KT * T * 4
    RC = RB + 2 * KT * T * 4
    REND = RC + KT * T * 4
    act_a = [at(f"act_a_{n}", [P, KT, T], F32R, RA + i * KT * T * 4) for i, n in enumerate(("hi", "lo"))]
    act_b = [at(f"act_b_{n}", [P, KT, T], F32R, RB + i * KT * T * 4) for i, n in enumerate(("hi", "lo"))]
    acc = at("acc", [P, KT, T], F32, RC)

    def region(start, end, *items):
        out, o = [], start
        for name, shape, dt in items:
            out.append(at(name, shape, dt, o))
            o = (plan[name][1] + 31) // 32 * 32
        assert o <= end, (items[0][0], o, end)
        return out

    (rows_conv, rows_vec, rows_hist, rows_pool, ada0, ada1, xin0, xin1, junk, hf0, hf1, z0, z1, raw0, raw1, cv0, cv1,
     wdt_raw, wdt_hi, wdt_lo, dt_row, dt_in, dt_e, dt_s, dt_q, dt_p) = region(
        RB, REND,
        ("rows_conv", [5 * CT, P], F32), ("rows_vec", [104, P], F32), ("rows_hist", [3 * CT, P], F32),
        ("rows_pool", [PW * KT, P], F32),
        ("ada0", [P, KT, 256], F32), ("ada1", [P, KT, 256], F32),
        ("xin0", [P, D], F32), ("xin1", [P, D], F32), ("junk", [P, D], F32),
        ("hf0", [P, KT, P], F32), ("hf1", [P, KT, P], F32),
        ("zb0", [P, T + DEC], F32), ("zb1", [P, T + DEC], F32),
        ("raw0", [P, 1160], F32), ("raw1", [P, 1160], F32), ("cv0", [P, T + 3 + DEC], F32), ("cv1", [P, T + 3 + DEC], F32),
        ("wdt_raw", [P, KT * HEADS], F32), ("wdt_hi", [P, KT * HEADS], F32R), ("wdt_lo", [P, KT * HEADS], F32R),
        ("dt_row", [HEADS, T], F32), ("dt_in", [P, NCH, HEADS], F32), ("dt_e", [P, NCH, HEADS], F32),
        ("dt_s", [P, NCH, HEADS], F32), ("dt_q", [P, NCH, HEADS], F32), ("dt_p", [P, NCH, HEADS], F32))
    o_end = (plan["dt_p"][1] + 31) // 32 * 32
    (acs_row,) = region(plan["hf0"][0], plan["hf1"][1], ("acs_row", [HEADS, NCH * CH], F32))
    (ada_sum,) = region(o_end, REND, ("ada_sum", [P, ADA_DVE, 2, 256], F32))
    ada, xin, hf, zb, raw, cv = [ada0, ada1], [xin0, xin1], [hf0, hf1], [z0, z1], [raw0, raw1], [cv0, cv1]
    wdt = [wdt_hi, wdt_lo]

    ada_first = region(RA, RB, *[(f"ada_first{k}", [P, KT, 256], F32) for k in range(8)])

    y_in0, ysq, rms_v, rms_g = region(
        RB, RC, ("y_in0", [P, 4, T], F32), ("ysq", [P, 4, T], F32), ("rms_v", [P, NCH], F32), ("rms_g", [P, NCH], F32))
    ssd_at = (plan["rms_g"][1] + 31) // 32 * 32
    s = region(
        ssd_at, REND,
        *[(f"xs_in{i}", [P, 4, CH], F32) for i in range(3)], *[(f"bc_in{i}", [P, 2, CH], F32) for i in range(3)],
        *[(f"z_in{i}", [P, 4, CH], F32) for i in range(3)], *[(f"acs_in{i}", [P, HPG, CH], F32) for i in range(3)],
        ("gp0", [P, T], F32), ("gp1", [P, T], F32),
        ("x_dt", [P, HPG, HD], F32), ("x_end", [P, HPG, HD], F32), ("b_tok", [P, NS], F32), 
        ("decay", [P, HPG, CH], F32), ("mix", [P, HPG, CH], F32), ("state", [P, HPG, HD], F32),
        ("skip", [P, HPG, HD], F32), ("y_tok", [P, HPG, HD], F32), ("yg0", [P, 4, CH], F32), ("yg1", [P, 4, CH], F32),
        ("yg2", [P, 4, CH], F32),
        ("state_in", [P, 4, NS], F32), ("state_out0", [P, 4, NS], F32), ("state_out1", [P, 4, NS], F32))
    xs_in, bc_in, z_in, acs_in, gp = s[0:3], s[3:6], s[6:9], s[9:12], s[12:14]
    x_dt, x_end, b_tok, decay, mix, state, skip, y_tok = s[14:22]
    yg, state_in, state_out = s[22:25], s[25], s[26:28]

    pw_ = SEQ + DEC + 2 * PW
    y_in1, tail_rows, pool_x, pool_s0, pool_s1 = region(
        ssd_at, RC, ("y_in1", [P, 4, T], F32), ("tail_rows", [3 * CT, 2, P], F32),
        ("pool_x", [P, pw_], F32), ("pool_s0", [P, pw_], F32), ("pool_s1", [P, pw_], F32))
    y_in = [y_in0, y_in1]
    pooled_in = region(RB, RB + KT * T * 4, *[(f"pooled_in{i}", [P, 2, T], F32) for i in range(GROUPS)])
    gm = region(
        RA, RB, *[(f"pooled_{n}{i}", [P, 2, T], F32R) for i in range(2) for n in ("hi", "lo")])
    pooled = [gm[0:2], gm[2:4]]
    ga0, ga1, gb0, gb1, mg_t = region(
        RA, RB, *[(n, [P, T], F32) for n in ("ga0", "ga1", "gb0", "gb1")], ("mg_t", [P, T], F32))
    gates = [[ga0, gb0], [ga1, gb1]]
    n2_items = region(
        RA, RB, *[(n, [P, KT, P], F32) for n in ("xr0", "xr1", "sq_junk", "xn0", "xn1", "h20", "h21")],
        ("gate_row", [P, 2, D], F32), *[(f"wo_{n}_a", [P, 4, D], F32R) for n in ("hi", "lo")])
    xr, sq_junk, xn, h2, gate_row, wo_a = n2_items[0:2], n2_items[2], n2_items[3:5], n2_items[5:7], n2_items[7], n2_items[8:10]
    assert plan["mg_t"][1] <= plan["gate_row"][0]
    wo_c = region(RC, REND, *[(f"wo_{n}_c", [P, 4, D], F32R) for n in ("hi", "lo")])
    wo_res = [wo_a, wo_c]
    ff = region(RA, RB, *[(f"f_{n}{i}", [P, 2, T], F32R) for i in range(1) for n in ("hi", "lo")],
                ("silu_g", [P, T], F32), ("f_val", [P, T], F32))
    f_split = ff[0:2]
    silu_g, f_val = ff[2], ff[3]
    (fx0, fx1, fr0, fr1, fjunk, fo0, fo1, final_w) = region(
        RB, RC, *[(n, [P, KT, P], F32) for n in ("fx0", "fx1", "fr0", "fr1", "fjunk", "fo0", "fo1",
                                                  "final_w")])
    fx, fr, fo = [fx0, fx1], [fr0, fr1], [fo0, fo1]

    PS = nc.alloc_psum_tensor("PS", [P, 8, 512], F32)

    def dram(name, shape):
        return nc.dram_tensor(name, shape, F32, kind="Internal").ap()

    xs_c = dram("xs_c", (GROUPS * NCH, 4, P, CH))
    bc_c = dram("bc_c", (2, GROUPS * NCH, P, CH))
    z_c = dram("z_c", (GROUPS * NCH, 4, P, CH))
    acs_c = dram("acs_c", (GROUPS * NCH, HPG, CH))
    gp_s = dram("gp_s", (3 * KT, P, T))
    y_c = dram("y_c", (GROUPS * NCH, 4, P, CH))
    x2_s = dram("x2_s", (NCH, P, D))

    def S(name):
        return nc.alloc_semaphore(name)


    rows_in, consts, cols_ready, c_ready = S("rows_in"), S("consts"), S("cols_ready"), S("silu_c_ready")
    rows_t = S("rows_transposed")
    w_in_ = [S(f"w_landed{i}") for i in range(2)]
    hi_ready, lo_ready = S("w_hi_ready"), S("w_lo_ready")
    ada_in = [S(f"ada_landed{i}") for i in range(2)]
    ada_first_in = [S(f"ada_pair_landed{i}") for i in range(4)]
    ada_used, mods_mm, mods_ready = S("ada_summed"), S("mods_mm"), S("mods_ready")
    wdt_in, wdt_h, wdt_l = S("wdt_landed"), S("wdt_hi_ready"), S("wdt_lo_ready")
    dt_mm, dt_copied, dt_tok, dt_vec, dt_act = S("dt_mm"), S("dt_copied"), S("dt_tok"), S("dt_vec"), S("dt_act")
    dt_cum, acs_out = S("dt_cumsum"), S("acs_stored")
    mm, mm_free = {}, {}
    for ph in ("z", "xbc", "ssd", "brb", "pool", "bra", "out", "ffn"):
        mm[ph], mm_free[ph] = S(f"mm_{ph}"), S(f"bank_free_{ph}")
    z_store = [S(f"z_stored{i}") for i in range(2)]
    raw_hist = S("raw_hist")
    cv_step, cv_silu, cv_store = S("conv_step"), S("conv_silu"), [S(f"conv_stored{i}") for i in range(2)]
    chunk_in = [S(f"chunk_landed{i}") for i in range(3)]
    gp_store = [S(f"gp_stored{i}") for i in range(2)]
    y_store = [S(f"y_stored{i}") for i in range(3)]
    (ssd_a, ssd_b, ssd_c, decay_ready, masked, mask_turn, v_x, v_skip, v_b, v_xend, v_mix, v_y0, v_y1, y_ready, v_s0, state_ready,
     yg_ready, edge_t, edge_v, st_in) = [S(n) for n in (
         "ssd_tokens", "ssd_products", "ssd_turned", "decay_ready", "acs_masked", "mask_turn", "x_dt_ready", "skip_ready", "b_tok_ready",
         "x_end_ready", "mix_ready", "y_off_scaled", "y_summed", "y_ready", "state_decayed",
         "state_ready", "yg_ready", "edge_turned", "edge_copied", "state_landed")]
    edge_store = [S(f"state_stored{i}") for i in range(2)]
    y_back = [S(f"y_landed{i}") for i in range(2)]
    ysq_ready, gs_mm, rms_vec, rms_pow, rms_wide, yn_ready, yb_hi, yb_lo = [S(n) for n in (
        "ysq_ready", "group_sum", "group_variance", "group_rms", "rms_spread", "y_normed", "y_hi", "y_lo")]
    tails_t, tails_v, tails_out = S("tails_turned"), S("tails_copied"), S("tails_stored")
    pool_x_in, pooled_back = S("pool_x_landed"), [S(f"pooled_landed{i}") for i in range(2)]
    pl_vec, pl_store, pm_h, pm_l, ab_hi, pl_set = [S(n) for n in (
        "pool_vec", "pooled_stored", "pooled_hi", "pooled_lo", "a_hi", "pool_set")]
    ptail_t, ptail_v, ptail_out = S("pool_tails_turned"), S("pool_tails_copied"), S("pool_tails_stored")
    gate_in = [S(f"gate_landed{i}") for i in range(2)]
    gate_tanh, mg_vec, mg_hi, mg_lo = S("gate_tanh"), S("merge_vec"), S("merged_hi"), S("merged_lo")
    f_silu, f_hi, f_lo = S("ffn_silu"), S("ffn_hi"), S("ffn_lo")
    y_add, gates_wide, gates_row = S("acc_cleared"), S("gate1_spread"), S("gate1_row")
    out_sem, x2_out = [S(f"y_out{i}") for i in range(2)], [S(f"x2_stored{i}") for i in range(2)]

    class Norm:
        def __init__(self, n, turned_in, modulates):
            self.landed = [S(f"{n}_landed{i}") for i in range(2)]
            self.squared, self.var, self.rms, self.scaled = [S(f"{n}_{k}") for k in ("squared", "var", "rms", "scaled")]
            if turned_in:
                self.turned_in = S(f"{n}_turned_in")
            if n != "norm1":
                self.added = S(f"{n}_added")
            if modulates:
                self.turned, self.modulated, self.hi, self.lo = [
                    S(f"{n}_{k}") for k in ("turned", "modulated", "hi", "lo")]

    n1, n2, n3 = Norm("norm1", False, True), Norm("norm2", False, True), Norm("norm3", True, False)
    fw_in = S("final_w_landed")

    def kmaj(w):
        return w.rearrange("(k p) n -> p k n", p=P)

    x_p, x_s = A["x_prompt"][0], A["x_sample"][0]
    yo_p, yo_s = O[0][0], O[1][0]
    win, wada = kmaj(A["w_in"][0]), kmaj(A["w_ada"][0])
    U_SSD, U_B = 40, 64
    U_POOL = U_B + 16
    U_A = U_POOL + 2
    U_OUT = U_A + 8
    U_FFN = U_OUT + 8
    U_END = U_FFN + 6 * FG
    FFN_SUBS, FFN_DVE = 36 * FG, 30 * FG
    DV_DTA, DV_TAB, N_ROWS, N_MEMSET = 19, 26, 14, 3 + PW + 1 + 6
    POLY = [1.0 / (2 * k + 1) for k in range(9)]

    def bank(b):
        return PS[:, b, :]

    def banks2(b, n=P):
        return PS[:, b:b + 2, :].rearrange("p b (f l) -> p (b f) l", l=P)

    def hb(tab, c, g):
        return tab[:, c, :][:, ds(g * HPG, HPG)].unsqueeze(2).broadcast_to([P, HPG, HD])

    PL_DONE = []
    for j in range(KT):
        PL_DONE.append((PL_DONE[-1] if j else 0) + 3 + (j // 2 + 1) + 4)

    blk = nc.Block()
    with blk as block:
        @block.sync
        def _(sp):
            def load_unit(u, v, src, first=False):
                if not first:
                    sp.wait_ge(lo_ready, u - 1)
                sp.dma_start(w_raw[v][:, :].rearrange("p (k n) -> p k n", n=src.shape[-1]), src).then_inc(w_in_[v], 16)

            def vec(w):
                return w.rearrange("(t c) -> t c", c=P)

            rows = [(rows_conv[0:4 * CT, :], A["conv_w"][0].rearrange("k (t c) -> (k t) c", c=P)),
                    (rows_conv[4 * CT:5 * CT, :], vec(A["conv_b"][0])),
                    (rows_vec[0:48, :], vec(A["b_ada"][0])), (rows_vec[48:56, :], vec(A["norm1_w"][0])),
                    (rows_vec[56:64, :], vec(A["norm2_w"][0])), (rows_vec[64:72, :], vec(A["pool_scale"][0])),
                    (rows_vec[72:88, :], vec(A["ssm_norm_w"][0])), (rows_vec[88:96, :], vec(A["c_prompt"][0])),
                    (rows_vec[96:104, :], vec(A["c_sample"][0])),
                    (rows_hist[:, :], A["state_conv"][0, 0].rearrange("k (t c) -> (k t) c", c=P)),
                    (rows_pool[:, :], A["state_pool"][0, 0].rearrange("k (t c) -> (k t) c", c=P)),
                    (bc_head[:, 0, :], A["dt_bias"][0].partition_broadcast(P)),
                    (bc_head[:, 1, :], A["a_log"][0].partition_broadcast(P)),
                    (bc_head[:, 2, :], A["d_skip"][0].partition_broadcast(P))]
            assert len(rows) == N_ROWS
            for dst, src in rows:
                sp.dma_start(dst, src).then_inc(rows_in, 16)
            for k in range(2):
                sp.dma_start(xin[k][:, :], x_p[k * P:(k + 1) * P, :]).then_inc(n1.landed[k], 16)
            for k in range(8):
                sp.dma_start(ada_first[k][:, :, :], wada[:, :, k * 256:(k + 1) * 256]).then_inc(ada_first_in[k // 2], 16)
            sp.dma_start(wdt_raw[:, :].rearrange("p (k n) -> p k n", n=HEADS),
                         win[:, :, COL_DT:COL_DT + HEADS]).then_inc(wdt_in, 16)
            for v in range(2):
                load_unit(v, v, win[:, :, COL_Z + v * P:COL_Z + (v + 1) * P], first=True)
            with sp.Fori(1, 4) as i:
                for v in range(2):
                    sp.wait_ge(n1.turned, i * 2 + v - 1)
                    sp.dma_start(xin[v][:, :], x_p[ds((i * 2 + v) * P, P), :]).then_inc(n1.landed[v], 16)
            sp.wait_ge(n1.turned, 7)
            sp.dma_start(xin[0][0:DEC, :], x_s).then_inc(n1.landed[0], 16)
            with sp.Fori(0, 8) as i:
                for v in range(2):
                    load_unit(i * 2 + v + 2, v, win[:, :, ds((i * 2 + v + 2) * P + COL_Z, P)])
                    sp.wait_ge(ada_used, (i * 2 + v) * 16 + ADA_DVE * 16 - 16)
                    sp.dma_start(ada[v][:, :, :], wada[:, :, ds((i * 2 + v + 8) * 256, 256)]).then_inc(ada_in[v], 16)
            with sp.Fori(0, 11) as i:
                for v in range(2):
                    load_unit(i * 2 + v + 18, v, win[:, :, ds((i * 2 + v + 2) * P + COL_XBC, P)])

            wba, wbb, wo = kmaj(A["w_branch_a"][0]), kmaj(A["w_branch_b"][0]), kmaj(A["w_out"][0])

            def y_out(t, k):
                sp.dma_start(y_c[t].rearrange("f p l -> p f l"), yg[k][:, :, :]).then_inc(y_store[k], 16)

            def y_again(g):
                if g >= 2:
                    sp.wait_ge(yb_lo, 4 * (g - 1))
                for f in range(4):
                    sp.dma_start(y_in[g % 2][:, f, 0:SEQ].rearrange("p (c l) -> p c l", l=CH),
                                 y_c[g * NCH:g * NCH + 8, f].rearrange("c p l -> p c l")).then_inc(y_back[g % 2], 16)
                sp.dma_start(y_in[g % 2][:, :, SEQ:T], y_c[g * NCH + 8, :, :, 0:DEC].rearrange("f p l -> p f l"))\
                  .then_inc(y_back[g % 2], 16)

            def chunk_loads(b, first=False):
                for k in range(3):
                    t = b * 3 + k
                    sp.wait_ge(yg_ready, t + 1)
                    if not first:
                        y_out(t - 3, k)
                    sp.dma_start(xs_in[k][:, :, :], xs_c[t].rearrange("f p l -> p f l")).then_inc(chunk_in[k], 16)
                    sp.dma_start(bc_in[k][:, :, :], bc_c.rearrange("b t p l -> t p b l")[t]).then_inc(chunk_in[k], 16)
                    sp.dma_start(z_in[k][:, :, :], z_c[t].rearrange("f p l -> p f l")).then_inc(chunk_in[k], 16)
                    sp.dma_start(acs_in[k][:, :, :], acs_c[t].partition_broadcast(P)).then_inc(chunk_in[k], 16)

            for v in range(2):
                load_unit(U_SSD + v, v, win[:, :, v * P:(v + 1) * P])
            sp.wait_ge(acs_out, 16 * GROUPS)
            for q in range(2):
                sp.wait_ge(z_store[q], 8 * 32)
                sp.wait_ge(cv_store[q], 12 * 32)
            sp.wait_ge(cv_silu, CT)
            chunk_loads(0, first=True)
            for v in range(2):
                load_unit(U_SSD + 2 + v, v, win[:, :, (2 + v) * P:(3 + v) * P])
            with sp.Fori(1, 3) as b:
                chunk_loads(b)
                for v in range(2):
                    load_unit(b * 2 + v + U_SSD + 2, v, win[:, :, ds((b * 2 + v + 2) * P, P)])
            with sp.Fori(3, 11) as b:
                chunk_loads(b)
                for v in range(2):
                    load_unit(b * 2 + v + U_SSD + 2, v, win[:, :, ds((b * 2 + v + 2 - KT) * P + COL_GATES, P)])
            for k in range(3):
                sp.wait_ge(y_store[k], 10 * 16)
            y_again(0)
            chunk_loads(11)
            load_unit(U_B, 0, wbb[:, 0:4, 0:256])
            for k in range(3):
                sp.wait_ge(yg_ready, 33 + k + 4)
                y_out(33 + k, k)
            for k in range(3):
                sp.wait_ge(y_store[k], 12 * 16)
            load_unit(U_B + 1, 1, wbb[:, 0:4, 256:512])
            sp.wait_ge(edge_t, 12)
            sp.wait_ge(edge_v, 8)
            for q in range(2):
                sp.wait_ge(edge_store[q], 16 * GROUPS)
                sp.wait_ge(gp_store[q], 12 * 16)

            for g in range(GROUPS):
                if g < GROUPS - 1:
                    y_again(g + 1)
                for q in range(4):
                    u = 4 * g + q + 2
                    if u < 16:
                        load_unit(U_B + u, u % 2, wbb[:, 4 * (u // 4):4 * (u // 4) + 4, (u % 4) * 256:(u % 4 + 1) * 256])
            wpg = A["pool_group_w"][0].rearrange("g c d -> (g c) d").rearrange("(q p) n -> p q n", p=P)
            for v in range(2):
                load_unit(U_POOL + v, v, wpg[:, 4 * v:4 * v + 4, :])
            for gi in range(GROUPS):
                sp.wait_ge(yb_lo, 4 * (gi // 2) + 12)
                sp.wait_ge(pl_store, 64 * (gi + 1))
                if gi >= 2:
                    sp.wait_ge(pm_h, 2 * gi - 2)
                for m in range(2):
                    sp.dma_start(pooled_in[gi][:, m, :], gp_s[2 * gi + m]).then_inc(pooled_back[gi % 2], 16)
                if gi == 1:
                    for v in range(2):
                        load_unit(U_A + v, v, wba[:, :, v * P:(v + 1) * P])

            def load_gates(m, v):
                sp.wait_ge(mg_vec, m * 5)
                for q in range(2):
                    sp.dma_start(gates[v][q][:, :], gp_s[m + (1 + q) * KT]).then_inc(gate_in[v], 16)

            sp.wait_ge(mm_free["pool"], 3 * KT + 3)
            with sp.Fori(0, 3) as i:
                for v in range(2):
                    load_gates(i * 2 + v, v)
                    load_unit(i * 2 + v + U_A + 2, v, wba[:, :, ds((i * 2 + v + 2) * P, P)])
            for v in range(2):
                load_gates(6 + v, v)
                load_unit(U_OUT + v, v, wo[:, v:v + 1, :])
            for k in range(2, KT):
                load_unit(U_OUT + k, k % 2, wo[:, k:k + 1, :])
            wg, wu, wd = kmaj(A["w_ffn_gate"][0]), kmaj(A["w_ffn_up"][0]), kmaj(A["w_ffn_down"][0])
            load_unit(U_FFN, 0, wg[:, :, 0:P])
            load_unit(U_FFN + 1, 1, wu[:, :, 0:P])
            def again_x(t, v, i, L=CH):
                if i is not None:
                    sp.wait_ge(x2_out[v], i * 16)
                    sp.wait_ge(n2.scaled, t - 1)
                src = x_s if L == DEC else x_p[ds(t * P, P), :]
                sp.dma_start(xr[v][0:L, :, :], src.rearrange("t (f c) -> t f c", c=P)).then_inc(n2.landed[v], 16)

            sp.wait_ge(mg_vec, 5 * KT + 5)
            for v in range(2):
                again_x(v, v, None)
            with sp.Fori(1, 4) as i:
                for v in range(2):
                    again_x(i * 2 + v, v, i)
            again_x(8, 0, 4, DEC)
            load_unit(U_FFN + 2, 0, wg[:, :, P:2 * P])
            load_unit(U_FFN + 3, 1, wu[:, :, P:2 * P])
            with sp.Fori(1, FG) as i:
                u0 = i * 6 + (U_FFN - 2)
                load_unit(u0, 0, wg[:, :, ds(i * 2 * P, P)])
                load_unit(u0 + 1, 1, wu[:, :, ds(i * 2 * P, P)])
                for v in range(2):
                    load_unit(u0 + 2 + v, v, wd[:, ds(i * 2 - 2, 2), v * 512:(v + 1) * 512])
                load_unit(u0 + 4, 0, wg[:, :, ds(i * 2 * P + P, P)])
                load_unit(u0 + 5, 1, wu[:, :, ds(i * 2 * P + P, P)])
            for v in range(2):
                load_unit(U_END - 2 + v, v, wd[:, 2 * FG - 2:2 * FG, v * 512:(v + 1) * 512])
            sp.wait_ge(mm["ffn"], FFN_SUBS)
            sp.dma_start(final_w[:, :, :], A["final_norm_w"].rearrange("(f c) -> f c", c=P).partition_broadcast(P))\
              .then_inc(fw_in, 16)

            def x2_again(t, v, L=CH, first=False):
                if not first:
                    sp.wait_ge(n3.added, t - 1)
                sp.dma_start(fr[v][0:L, :, :], x2_s[t][0:L, :].rearrange("t (f c) -> t f c", c=P))\
                  .then_inc(n3.landed[v], 16)

            def y_final(t, v, L=CH):
                sp.wait_ge(n3.scaled, t + 1)
                dst = yo_s if L == DEC else yo_p[ds(t * P, P), :]
                sp.dma_start(dst.rearrange("t (f c) -> t f c", c=P), fo[v][0:L, :, :]).then_inc(out_sem[v], 16)

            for v in range(2):
                x2_again(v, v, first=True)
            with sp.Fori(1, 4) as i:
                for v in range(2):
                    x2_again(i * 2 + v, v)
                for v in range(2):
                    y_final(i * 2 + v - 2, v)
            x2_again(8, 0, DEC)
            for v in range(2):
                y_final(6 + v, v)
            y_final(8, 0, DEC)
            for v in range(2):
                sp.wait_ge(out_sem[v], 16 * (5 - v))

        @block.gpsimd
        def _(pool):
            pool.memset(ones[:, :], 1.0).then_inc(consts, 1)
            pool.memset(ident[:, :], 0.0).then_inc(consts, 1)
            pool.memset(half[:, :], -0.5).then_inc(consts, 1)
            for k in range(PW):
                pool.memset(inv_pos[:, k:k + 1], 1.0 / (k + 1)).then_inc(consts, 1)
            pool.memset(dt_in[:, :, :], 0.0).then_inc(consts, 1)
            for v in range(2):
                pool.memset(raw[v][:, 0:3], 0.0).then_inc(consts, 1)
                pool.memset(zb[v][:, T:T + DEC], 0.0).then_inc(consts, 1)
                pool.memset(cv[v][:, T + 3:T + 3 + DEC], 0.0).then_inc(consts, 1)
            pool.wait_ge(consts, N_MEMSET)
            pool.affine_select(out=ident[:, :], in_=ident[:, :], compare_op=ALU.not_equal, fill=1.0, base=0,
                               pattern=[[-1, P]], channel_multiplier=1).then_inc(consts, 1)
            pool.affine_select(out=upper[:, :], in_=ones[:, :], compare_op=ALU.is_ge, fill=0.0, base=0,
                               pattern=[[1, P]], channel_multiplier=-1).then_inc(consts, 1)

            def powers(n, t, v, L=P):
                pool.wait_ge(n.var, t + 1)
                pool.tensor_tensor(small[0:L, 4 + v:5 + v], small[0:L, 2 + v:3 + v], half[0:L, 0:1], ALU.pow)\
                    .then_inc(n.rms, 1)

            with pool.Fori(0, 4) as i:
                for v in range(2):
                    powers(n1, i * 2 + v, v)
            powers(n1, 8, 0, DEC)
            ssm_in = A["state_ssm"][0, 0].rearrange("h p n -> (h p) n").rearrange("(g i q) n -> g q i n", g=GROUPS, q=P)
            ssm_out = [O[k][0, 0].rearrange("h p n -> (h p) n").rearrange("(g i q) n -> g q i n", g=GROUPS, q=P)
                       for k in (4, 7)]
            pool.wait_ge(cv_silu, CT)
            for q in range(2):
                pool.wait_ge(cv_store[q], 12 * 32)

            def causal(g, j, k):
                pool.wait_ge(chunk_in[k], (g * 3 + j) * 64 + 64)
                pool.sem_inc(mask_turn, 1)
                pool.affine_select(out=acs_in[k][:, :, :], in_=acs_in[k][:, :, :], compare_op=ALU.is_ge, fill=-1e30,
                                   base=0, pattern=[[0, HPG], [1, CH]], channel_multiplier=-1).then_inc(masked, 1)

            def store_state(q, g):
                pool.wait_ge(edge_v, g * 2 + q + 1)
                pool.dma_start(ssm_out[q][g], state_out[q][:, :, :]).then_inc(edge_store[q], 16)

            for g in range(GROUPS):
                for k in range(3):
                    causal(g, 0, k)
                if g:
                    store_state(1, g - 1)
                    pool.wait_ge(edge_t, g * 3)
                pool.dma_start(state_in[:, :, :], ssm_in[g]).then_inc(st_in, 16)
                with pool.Fori(1, 3) as j:
                    for k in range(3):
                        causal(g, j, k)
                store_state(0, g)
            store_state(1, GROUPS - 1)
            def tokens_rms(g):
                if g:
                    pool.wait_ge(rms_wide, g)
                pool.wait_ge(rms_vec, 2 * g + 2)
                for r, c in [(P, slice(0, NCH - 1)), (DEC, slice(NCH - 1, NCH))]:
                    w_ = c.stop - c.start
                    pool.tensor_tensor(rms_g[0:r, c], rms_v[0:r, c], half[0:r, 0:1].broadcast_to([r, w_]), ALU.pow)\
                        .then_inc(rms_pow, 1)

            tokens_rms(0)
            pool.wait_ge(tails_v, 2)
            for q, k in enumerate((3, 6)):
                pool.dma_start(O[k][0, 0].rearrange("k (t c) -> (k t) c", c=P), tail_rows[:, q, :]).then_inc(tails_out, 16)
            at_s = SEQ + 2 * PW

            def pool_in(j):
                if j:
                    pool.wait_ge(pl_vec, PL_DONE[j - 1])
                pool.dma_start(pool_x[:, PW:PW + SEQ], gp_s[j][:, 0:SEQ]).then_inc(pool_x_in, 16)
                pool.dma_start(pool_x[:, at_s:at_s + DEC], gp_s[j][:, SEQ:T]).then_inc(pool_x_in, 16)

            def pool_out(j):
                pool.wait_ge(pl_vec, PL_DONE[j])
                src = [pool_s0, pool_s1][(j // 2) % 2]
                pool.dma_start(gp_s[j][:, 0:SEQ], src[:, PW:PW + SEQ]).then_inc(pl_store, 16)
                pool.dma_start(gp_s[j][:, SEQ:T], src[:, at_s:at_s + DEC]).then_inc(pl_store, 16)

            pool.wait_ge(edge_t, 12)
            pool.wait_ge(edge_v, 8)
            for q in range(2):
                pool.wait_ge(edge_store[q], 16 * GROUPS)
                pool.wait_ge(gp_store[q], 12 * 16)
            for k in range(3):
                pool.wait_ge(y_store[k], 12 * 16)
            pool_in(0)
            for g in range(GROUPS):
                pool_out(2 * g)
                pool_in(2 * g + 1)
                if g < GROUPS - 1:
                    tokens_rms(g + 1)
                pool_out(2 * g + 1)
                if g < GROUPS - 1:
                    pool_in(2 * g + 2)
            pool.wait_ge(ptail_v, 2)
            for q, k in enumerate((2, 5)):
                pool.dma_start(O[k][0, 0].rearrange("k (t c) -> (k t) c", c=P), pool_rows[:, q, :]).then_inc(ptail_out, 16)
            def pairs(body):
                with pool.Fori(0, 4) as i:
                    body([(i * 2, 0, i), (i * 2 + 1, 1, i)], CH)
                body([(8, 0, 4)], DEC)

            def norm2_tiles(tiles, L):
                for t, v, i in tiles:
                    powers(n2, t, v, L)

            def norm3_tiles(tiles, L):
                for t, v, i in tiles:
                    powers(n3, t, v, L)

            pairs(norm2_tiles)
            pool.wait_ge(mm["out"], NCH)
            pool.memset(acc[:, :, :], 0.0).then_inc(y_add, 1)
            pairs(norm3_tiles)
            for sem, n in [(edge_store[0], 4), (edge_store[1], 4), (tails_out, 2), (ptail_out, 2)]:
                pool.wait_ge(sem, 16 * n)

        @block.scalar
        def _(act):
            def hi(u, v, ph, done):
                act.wait_ge(w_in_[v], (u - v) * 8 + 16)
                act.wait_ge(mm[ph], done)
                act.activation(w_split[v][0][:, :], w_raw[v][:, :], ACT.Copy).then_inc(hi_ready, 1)

            def hi_out(k):
                v = k % 2
                act.wait_ge(w_in_[v], (U_OUT + k - v) * 8 + 16)
                act.activation(wo_res[k // 4][0][:, k % 4, :], w_raw[v][:, :], ACT.Copy).then_inc(hi_ready, 1)

            act.wait_ge(cols_ready, 4)
            act.activation(silu_c[:, :, :].rearrange("p k s -> p s k"),
                           cols_vec[:, 88:104].rearrange("p (s k) -> p s k", s=2), ACT.Silu).then_inc(c_ready, 1)
            act.wait_ge(rows_in, 16 * N_ROWS)
            act.activation(bc_head[:, 1, :], bc_head[:, 1, :], ACT.Exp).then_inc(c_ready, 1)

            def squares(n, src, jk, v, t, L=P):
                act.wait_ge(n.squared, t)
                act.activation(jk[0:L], src[0:L], ACT.Square, accum_out=small[0:L, v:v + 1]).then_inc(n.squared, 1)

            def norm1_first(t, v, L):
                act.wait_ge(n1.landed[v], (t - v) * 8 + 16)
                squares(n1, xin[v][:, :], junk[:, :], v, t, L)

            def norm1_hi(t, v, L):
                act.wait_ge(n1.modulated, t + 3)
                act.activation(act_a[0][:, :, ds(t * P, L)], hf[v][:, :, 0:L], ACT.Copy).then_inc(n1.hi, 1)

            def norm1_scale(t, v, L):
                act.wait_ge(n1.rms, t + 1)
                act.activation(xin[v][0:L, :], xin[v][0:L, :], ACT.Copy, scale=small[0:L, 4 + v:5 + v]).then_inc(n1.scaled, 1)

            def norm1_step(t, v, L=CH):
                norm1_first(t, v, L)
                norm1_hi(t - 1, 1 - v, CH)
                norm1_scale(t, v, L)

            norm1_first(0, 0, CH)
            norm1_scale(0, 0, CH)
            hi(0, 0, "z", 0)
            act.wait_ge(wdt_in, 16)
            act.activation(wdt[0][:, :], wdt_raw[:, :], ACT.Copy).then_inc(wdt_h, 1)
            with act.Fori(0, 3) as i:
                norm1_step(i * 2 + 1, 1)
                norm1_step(i * 2 + 2, 0)
            norm1_step(7, 1)
            norm1_step(8, 0, DEC)
            norm1_hi(8, 0, DEC)
            for n, (o, w) in enumerate(SUBS):
                act.wait_ge(dt_mm, n + 1)
                act.activation(dt_row[:, o:o + w], PS[0:HEADS, n, 0:w], ACT.Copy).then_inc(dt_copied, 1)
            act.wait_ge(dt_vec, 2)
            act.activation(dt_q[:, :, :], dt_in[:, :, :], ACT.Abs).then_inc(dt_act, 1)
            act.wait_ge(dt_act, 1)
            act.activation(dt_e[:, :, :], dt_q[:, :, :], ACT.Exp, scale=-1.0).then_inc(dt_act, 1)

            act.sem_inc(mm_free["z"], 3)
            zv = z_c.rearrange("(g c) f p l -> g f p c l", g=GROUPS)
            with act.Fori(0, GROUPS) as g:
                with act.Fori(0, 2) as i:
                    for v in range(2):
                        u = g * 4 + i * 2 + v
                        hi(u + 1, 1 - v, "z", u * 3)
                        act.wait_ge(z_store[v], (g * 2 + i) * 32)
                        for n, (o, w) in enumerate(SUBS):
                            act.wait_ge(mm["z"], u * 3 + n + 1)
                            act.activation(zb[v][:, o:o + w], PS[:, n, 0:w], ACT.Silu).then_inc(mm_free["z"], 1)
                        act.wait_ge(mm_free["z"], u * 3 + 6)
                        dst = zv[g][i * 2 + v]
                        act.dma_start(dst[:, 0:NCH - 1, :], zb[v][:, 0:SEQ].rearrange("p (c l) -> p c l", l=CH))\
                           .then_inc(z_store[v], 16)
                        act.dma_start(dst[:, NCH - 1, :], zb[v][:, SEQ:SEQ + CH]).then_inc(z_store[v], 16)
            act.wait_ge(dt_vec, DV_TAB)
            act.activation(eacs_tab[:, :, :], dt_s[:, :, :], ACT.Exp).then_inc(dt_act, 1)
            act.activation(dend_tab[:, :, :], dt_e[:, :, :], ACT.Exp).then_inc(dt_act, 1)
            act.activation(bdec_tab[:, :, :], dt_p[:, :, :], ACT.Exp).then_inc(dt_act, 1)
            for g in range(GROUPS):
                act.dma_start(acs_c[g * NCH:(g + 1) * NCH].rearrange("c h l -> h c l"),
                              acs_row[g * HPG:(g + 1) * HPG, :].rearrange("h (c l) -> h c l", l=CH)).then_inc(acs_out, 16)
            act.sem_inc(mm_free["xbc"], 3)

            def conv_tile(n_, v, dst):
                u = n_ + 16
                hi(u + 1, 1 - v, "xbc", n_ * 3)
                act.wait_ge(cv_step, n_ * 4 + 4)
                for n, (o, w) in enumerate(SUBS):
                    act.wait_ge(mm["xbc"], n_ * 3 + n + 1)
                    if n < 2:
                        act.activation(raw[v][:, 3 + o:3 + o + w], PS[:, n, 0:w], ACT.Copy).then_inc(mm_free["xbc"], 1)
                    else:
                        act.activation(raw[v][:, 3 + o:3 + SEQ], PS[:, n, 0:SEQ - o], ACT.Copy)
                        act.activation(raw[v][:, 6 + SEQ:6 + T], PS[:, n, SEQ - o:w], ACT.Copy).then_inc(mm_free["xbc"], 1)
                act.wait_ge(cv_step, n_ * 4 + 12)
                act.activation(cv[v][:, 0:T + 3], cv[v][:, 0:T + 3], ACT.Silu).then_inc(cv_silu, 1)
                act.wait_ge(cv_silu, n_ + 1)
                act.dma_start(dst[:, 0:NCH - 1, :], cv[v][:, 0:SEQ].rearrange("p (c l) -> p c l", l=CH))\
                   .then_inc(cv_store[v], 16)
                act.dma_start(dst[:, NCH - 1, :], cv[v][:, SEQ + 3:SEQ + 3 + CH]).then_inc(cv_store[v], 16)

            xv = xs_c.rearrange("(g c) f p l -> g f p c l", g=GROUPS)
            bv = bc_c.rearrange("b (g c) p l -> b g p c l", g=GROUPS)
            with act.Fori(0, GROUPS) as g:
                with act.Fori(0, 2) as i:
                    for v in range(2):
                        conv_tile(g * 4 + i * 2 + v, v, xv[g][i * 2 + v])
            with act.Fori(0, 2) as b:
                with act.Fori(0, 2) as i:
                    for v in range(2):
                        conv_tile(b * 4 + i * 2 + v + 16, v, bv[b][i * 2 + v])

            act.sem_inc(mm_free["ssd"], 3)
            act.wait_ge(cv_store[0], 12 * 32)
            act.wait_ge(cv_store[1], 12 * 32)
            act.wait_ge(z_store[0], 8 * 32)
            act.wait_ge(z_store[1], 8 * 32)
            act.wait_ge(acs_out, 16 * GROUPS)

            def decays(g, j, k):
                t = g * NCH + j * 3 + k
                act.wait_ge(masked, t + 1)
                act.wait_ge(v_mix, t)
                for h in range(HPG):
                    e = act.activation(decay[:, h, :], acs_in[k][:, h, :], ACT.Exp,
                                       bias=nacs_tab[:, :, :].rearrange("p c h -> p (c h)")
                                       [:, ds((j * 3 + k) * HEADS + g * HPG + h, 1)])
                e.then_inc(decay_ready, 1)

            def copy_third(b, q):
                v, n = divmod(q, 3)
                o, w = SUBS[n]
                if n == 0:
                    act.wait_ge(gp_store[v], b * 16)
                act.wait_ge(mm["ssd"], b * 6 + q + 1)
                act.activation(gp[v][:, o:o + w], PS[:, n, 0:w], ACT.Copy).then_inc(mm_free["ssd"], 1)
                if n == 2:
                    act.wait_ge(mm_free["ssd"], b * 6 + q + 4)
                    act.dma_start(gp_s[b * 2 + v], gp[v][:, :]).then_inc(gp_store[v], 16)

            def group_norm(g, piece):
                v = g % 2
                if piece == 0:
                    act.wait_ge(y_back[v], 80 * (g // 2 + 1))
                    if g:
                        act.wait_ge(gs_mm, g)
                    for f in range(4):
                        act.activation(ysq[:, f, :], y_in[v][:, f, :], ACT.Square).then_inc(ysq_ready, 1)
                if piece >= 2:
                    if piece == 2 and g >= 2:
                        act.wait_ge(mm["brb"], 24 * (g - 1))
                    for f in range(2 * piece - 4, 2 * piece - 2):
                        act.wait_ge(yn_ready, 4 * g + f + 1)
                        act.activation(act_a[0][:, 4 * v + f, :], y_in[v][:, f, :], ACT.Copy).then_inc(yb_hi, 1)

            def three_chunks(g, j, ahead):
                b = g * 3 + j
                hi(b * 2 + U_SSD + 1, 1, "ssd", b * 6)
                for k in range(3):
                    if k < 2:
                        decays(g, j, k + 1)
                    elif ahead:
                        decays(*ahead)
                    copy_third(b, 2 * k)
                    if k == 1:
                        hi(b * 2 + U_SSD + 2, 0, "ssd", b * 6 + 3)
                    copy_third(b, 2 * k + 1)

            def group(g, last):
                with act.Fori(0, 2) as j:
                    three_chunks(g, j, (g, j + 1, 0))
                if last:
                    group_norm(0, 0)
                three_chunks(g, 2, None if last else (g + 1, 0, 0))

            decays(0, 0, 0)
            with act.Fori(0, GROUPS - 1) as g:
                group(g, False)
            group(GROUPS - 1, True)

            act.wait_ge(mm["ssd"], 72)
            for piece in range(2, 4):
                group_norm(0, piece)
            for g in range(GROUPS):
                for q in range(4):
                    hi(U_B + 4 * g + q + 1, 1 - q % 2, "brb", 6 * (4 * g + q))
                    if g < GROUPS - 1:
                        group_norm(g + 1, q)
            def pooled_parts(gi):
                act.wait_ge(pooled_back[gi % 2], 32 * (gi // 2 + 1))
                if gi == 0:
                    act.wait_ge(mm["brb"], 4 * 24)
                if gi >= 2:
                    act.wait_ge(mm["pool"], 6 * (gi - 1))
                for m in range(2):
                    act.activation(pooled[gi % 2][0][:, m, :], pooled_in[gi][:, m, :], ACT.Copy).then_inc(pm_h, 1)

            def a_parts(gi):
                for m in range(2):
                    j = 2 * gi + m
                    for n, (o, w) in enumerate(SUBS):
                        act.wait_ge(mm["pool"], 3 * j + n + 1)
                        act.activation(act_b[0][:, j, o:o + w], PS[:, n, 0:w], ACT.Copy, scale=cols_vec[:, 64 + j:65 + j])\
                           .then_inc(ab_hi, 1)

            act.wait_ge(tails_out, 32)
            act.wait_ge(pl_store, 32 * KT)
            for gi in range(GROUPS):
                if gi == 0:
                    hi(U_POOL + 1, 1, "brb", 96)
                pooled_parts(gi)
                if gi:
                    a_parts(gi - 1)
                if gi == 2:
                    hi(U_A, 0, "pool", 12)
            a_parts(GROUPS - 1)
            act.wait_ge(mm_free["pool"], 3 * KT + 3)
            act.wait_ge(gates_wide, 1)
            act.activation(gate_row[:, :, :].rearrange("p s (b l) -> p (s b) l", l=512), PS[:, 4:8, :], ACT.Copy)\
               .then_inc(gates_row, 1)

            def tanh_gates(i, v):
                act.wait_ge(gate_in[v], i * 32 + 32)
                for q in range(2):
                    act.activation(gates[v][q][:, :], gates[v][q][:, :], ACT.Tanh, scale=0.5).then_inc(gate_tanh, 1)

            with act.Fori(0, 3) as i:
                for v in range(2):
                    hi(i * 2 + v + U_A + 1, 1 - v, "bra", i * 6 + 3 * v)
                    tanh_gates(i, v)
            hi(U_A + 7, 1, "bra", 18)
            tanh_gates(3, 0)
            tanh_gates(3, 1)
            for k in range(4):
                hi_out(k)
            act.wait_ge(mm["bra"], 3 * KT)
            for m in range(KT):
                act.wait_ge(mg_vec, 5 * m + 10)
                act.activation(act_b[0][:, m, :], acc[:, m, :], ACT.Copy, scale=0.5).then_inc(mg_hi, 1)
            act.wait_ge(mg_lo, KT)
            for k in range(4, KT):
                hi_out(k)
            hi(U_FFN, 0, "bra", 3 * KT)

            def norm2_first(t, v, L):
                act.wait_ge(n2.added, t + 1)
                act.dma_start(x2_s[t][0:L, :].rearrange("t (f c) -> t f c", c=P), xr[v][0:L, :, :]).then_inc(x2_out[v], 16)
                squares(n2, xr[v][:, :, :], sq_junk[:, :, :], v, t, L)

            def norm2_hi(t, v, L):
                act.wait_ge(n2.modulated, t + 3)
                act.activation(act_b[0][:, :, ds(t * P, L)], h2[v][:, :, 0:L], ACT.Copy).then_inc(n2.hi, 1)

            def norm2_scale(t, v, L):
                act.wait_ge(n2.rms, t + 1)
                act.activation(xn[v][0:L, :, :], xr[v][0:L, :, :], ACT.Copy, scale=small[0:L, 4 + v:5 + v])\
                   .then_inc(n2.scaled, 1)

            def norm2_step(t, v, L=CH):
                norm2_first(t, v, L)
                norm2_hi(t - 1, 1 - v, CH)
                norm2_scale(t, v, L)

            norm2_first(0, 0, CH)
            norm2_scale(0, 0, CH)
            with act.Fori(0, 3) as i:
                norm2_step(i * 2 + 1, 1)
                norm2_step(i * 2 + 2, 0)
            norm2_step(7, 1)
            norm2_step(8, 0, DEC)
            norm2_hi(8, 0, DEC)

            act.wait_ge(n2.lo, NCH)
            for q in range(2):
                act.wait_ge(x2_out[q], 16 * (5 - q))

            def gate_thirds(i, q, sub0):
                for n, (o, w) in enumerate(SUBS):
                    act.wait_ge(mm["ffn"], sub0 + n + 1)
                    act.activation(silu_g[:, o:o + w], PS[:, n, 0:w], ACT.Silu).then_inc(f_silu, 1)

            def f_part(q, dve_before):
                act.wait_ge(mm_free["ffn"], dve_before + 6)
                act.activation(f_split[0][:, q, :], f_val[:, :], ACT.Copy).then_inc(f_hi, 1)

            hi(U_FFN + 1, 1, "ffn", 0)
            gate_thirds(0, 0, 0)
            hi(U_FFN + 2, 0, "ffn", 3)
            f_part(0, 0)
            hi(U_FFN + 3, 1, "ffn", 6)
            gate_thirds(0, 1, 6)
            hi(U_FFN + 4, 0, "ffn", 9)
            f_part(1, 3)
            with act.Fori(1, FG) as i:
                u0, sub0, dve0 = i * 6 + (U_FFN - 2), i * 36 - 24, i * 30 - 24
                hi(u0 + 1, 1, "ffn", sub0)
                gate_thirds(i, 0, sub0)
                hi(u0 + 2, 0, "ffn", sub0 + 3)
                hi(u0 + 3, 1, "ffn", sub0 + 6)
                hi(u0 + 4, 0, "ffn", sub0 + 18)
                act.wait_ge(mm["ffn"], sub0 + 30)
                f_part(0, dve0)
                hi(u0 + 5, 1, "ffn", sub0 + 30)
                gate_thirds(i, 1, sub0 + 30)
                hi(u0 + 6, 0, "ffn", sub0 + 33)
                f_part(1, dve0 + 27)
            hi(U_END - 1, 1, "ffn", FFN_SUBS - 24)

            def norm3_squares(t, v, L=CH):
                act.wait_ge(n3.added, t + 1)
                squares(n3, fx[v][:, :, :], fjunk[:, :, :], v, t, L)

            act.wait_ge(mm_free["ffn"], FFN_DVE + 3)
            with act.Fori(0, 4) as i:
                for v in range(2):
                    norm3_squares(i * 2 + v, v)
            norm3_squares(8, 0, DEC)

        @block.tensor
        def _(pe):
            def thirds(ph, s0, v, steps, out_m=P, last=None):
                for n, (o, w) in enumerate(SUBS):
                    wait_bank(ph, s0, n)
                    for k, (wt, at_) in enumerate(steps):
                        for q, (a, b) in enumerate(PASSES):
                            e = pe.matmul(PS[0:out_m, n, 0:w], wt[a], at_[b][:, o:o + w],
                                          start=(k == 0 and q == 0), stop=(k == len(steps) - 1 and q == 2))
                    e.then_inc(mm[ph], 1)
                return e

            def wait_bank(ph, s0, n):
                pe.wait_ge(mm_free[ph], s0 + n + 1)

            def unit_ready(u):
                pe.wait_ge(lo_ready, u + 1)

            def cols(v, k, n, j=0, width=P):
                return [w_split[v][p][:, k * n + j:k * n + j + width] for p in range(2)]

            def tile_of(acts, k):
                return [acts[p][:, k, :] for p in range(2)]

            def full_unit(ph, u, s0, v, acts):
                unit_ready(u)
                thirds(ph, s0, v, [(cols(v, k, P), tile_of(acts, k)) for k in range(KT)])

            pe.wait_ge(consts, N_MEMSET + 2)
            pe.wait_ge(rows_in, 16 * N_ROWS)
            for q, (r, n) in enumerate([(rows_conv, 5 * CT), (rows_vec, 104), (rows_hist, 3 * CT), (rows_pool, PW * KT)]):
                e = pe.transpose(PS[:, 6, q * P:q * P + n], r[0:n, :], ident[0:n, 0:n])
            e.then_inc(rows_t, 1)

            def whole_slab(k):
                for j in range(2):
                    for q in range(KT):
                        e = pe.matmul(PS[:, 7, k * 4 + 2 * j:k * 4 + 2 * j + 2], ada_first[k][:, q, j * P:(j + 1) * P],
                                      silu_c[:, q, :], start=(q == 0), stop=(q == KT - 1))
                return e

            def summed_slab(k, slot):
                for j in range(2):
                    for s_ in range(2):
                        e = pe.matmul(PS[:, 7, ds(k * 4 + 2 * j + s_, 1)], ada_sum[:, slot, s_, j * P:(j + 1) * P],
                                      ones[:, 0:1], start=True, stop=True)
                e.then_inc(mods_mm, 1)

            pe.wait_ge(c_ready, 1)
            for k in ADA_WHOLE:
                pe.wait_ge(ada_first_in[k // 2], 32)
                e = whole_slab(k)
            e.then_inc(mods_mm, 1)
            for n, k in enumerate(ADA_SUMMED):
                pe.wait_ge(ada_used, 16 * n + 16)
                summed_slab(k, n)

            def pairs(body):
                with pe.Fori(0, 4) as i:
                    body([(i * 2, 0, i), (i * 2 + 1, 1, i)], CH)
                body([(8, 0, 4)], DEC)

            def turn(n, src, v, t, b, L):
                pe.wait_ge(n.scaled, t + 1)
                pe.wait_ge(n.modulated, t + 1)
                for f in range(KT):
                    e = pe.transpose(banks2(b)[:, f, 0:L], src[0:L, f, :], ident[0:L, 0:L])
                e.then_inc(n.turned, 1)

            def norm1_tiles(tiles, L):
                for t, v, i in tiles:
                    turn(n1, xin[v][:, :].rearrange("p (f c) -> p f c", c=P), v, t, 2 + 2 * v, L)

            pairs(norm1_tiles)
            pe.wait_ge(wdt_l, 1)
            for n, (o, w) in enumerate(SUBS):
                pe.wait_ge(n1.lo, 3 * n + 3)
                for k in range(KT):
                    for q, (a, b) in enumerate(PASSES):
                        e = pe.matmul(PS[0:HEADS, n, 0:w], wdt[a][:, k * HEADS:(k + 1) * HEADS], act_a[b][:, k, o:o + w],
                                      start=(k == 0 and q == 0), stop=(k == KT - 1 and q == 2))
                e.then_inc(dt_mm, 1)
            pe.wait_ge(dt_copied, 3)
            for c in range(NCH):
                L = CH if c < NCH - 1 else DEC
                e = pe.transpose(PS[0:L, 5, c * HEADS:(c + 1) * HEADS], dt_row[:, c * CH:c * CH + L],
                                 ident[0:HEADS, 0:HEADS])
            e.then_inc(dt_tok, 1)
            with pe.Fori(0, 8) as i:
                for v in range(2):
                    u = i * 2 + v
                    full_unit("z", u, u * 3, v, act_a)
                    pe.wait_ge(ada_used, u * 16 + (ADA_DVE + 1) * 16)
                    summed_slab(u + 8, v)
            pe.wait_ge(dt_vec, DV_DTA)
            dta = dt_q[:, :, :].rearrange("p c h -> p (c h)")
            pe.matmul(PS[:, 5, 0:NCH * HEADS], upper[:, :], dta, start=True, stop=True)
            pe.matmul(PS[:, 6, 0:NCH * HEADS], ones[:, :], dta, start=True, stop=True)
            for c in range(NCH):
                dst = PS[0:HEADS, 3 + c // 4, (c % 4) * CH:(c % 4 + 1) * CH] if c < 8 else PS[0:HEADS, 6, 384:512]
                e = pe.matmul(dst, dt_q[:, c, :], upper[:, :], start=True, stop=True)
            e.then_inc(dt_cum, 1)
            with pe.Fori(0, 12) as i:
                for v in range(2):
                    u = i * 2 + v
                    full_unit("xbc", u + 16, u * 3, v, act_a)

            def ssd_tokens(g, j, k):
                pe.wait_ge(chunk_in[k], (g * 3 + j) * 64 + 64)
                for f in range(4):
                    pe.transpose(PS[:, 3, f * P:(f + 1) * P], xs_in[k][:, f, :], ident[:, :])
                pe.transpose(PS[:, 4, 0:NS], bc_in[k][:, 0, :], ident[:, :])
                pe.matmul(PS[:, 4, P:2 * P], bc_in[k][:, 0, :], bc_in[k][:, 1, :], start=True, stop=True)\
                  .then_inc(ssd_a, 1)

            def ssd_products(g, j, k, c):
                t = g * NCH + j * 3 + k
                pe.wait_ge(yg_ready, t + 3)
                pe.wait_ge(state_ready, g * 11 + (j * 3 + k + 1 if c < 8 else 10))
                pe.matmul(PS[:, 6, :], bc_in[k][:, 1, :], state[:, :, :], start=True, stop=True)
                pe.wait_ge(v_xend, t + 1)
                pe.wait_ge(v_b, t + 1)
                pe.matmul(PS[:, 7, :], b_tok[:, :], x_end[:, :, :], start=True, stop=True)
                pe.wait_ge(v_mix, t + 1)
                for h in range(HPG):
                    e = pe.matmul(PS[:, 5, h * HD:(h + 1) * HD], mix[:, h, :], x_dt[:, h, :], start=True, stop=True)
                e.then_inc(ssd_b, 1)

            def ssd_turn(g, j, k):
                t = g * NCH + j * 3 + k
                pe.wait_ge(y_ready, t + 1)
                for f in range(4):
                    e = pe.transpose(PS[:, 6, f * P:(f + 1) * P], y_tok[:, 2 * f:2 * f + 2, :], ident[:, :])
                e.then_inc(ssd_c, 1)

            def third_of(b, q):
                v, n = divmod(q, 3)
                o, w = SUBS[n]
                if n == 0:
                    unit_ready(b * 2 + v + U_SSD)
                pe.wait_ge(mm_free["ssd"], b * 6 + q + 1)
                for k in range(KT):
                    for p_, (a, c) in enumerate(PASSES):
                        e = pe.matmul(PS[:, n, 0:w], w_split[v][a][:, k * P:(k + 1) * P], act_a[c][:, k, o:o + w],
                                      start=(k == 0 and p_ == 0), stop=(k == KT - 1 and p_ == 2))
                e.then_inc(mm["ssd"], 1)

            def state_turn(g, want):
                pe.wait_ge(state_ready, g * 11 + want)
                for f in range(4):
                    e = pe.transpose(PS[:, 7, f * P:(f + 1) * P], state[:, 2 * f:2 * f + 2, :], ident[:, :])
                e.then_inc(edge_t, 1)

            def ssd_step(g, j, k, c, ahead):
                b = g * 3 + j
                ssd_products(g, j, k, c)
                if ahead:
                    ssd_tokens(*ahead)
                third_of(b, 2 * k)
                ssd_turn(g, j, k)
                if c == NCH - 2:
                    state_turn(g, 9)
                    pe.wait_ge(st_in, g * 16 + 16)
                    for f in range(4):
                        e = pe.transpose(PS[:, 5, f * P:(f + 1) * P], state_in[:, f, :], ident[:, :])
                    e.then_inc(edge_t, 1)
                if c == NCH - 1:
                    state_turn(g, 11)
                third_of(b, 2 * k + 1)

            def group(g, last):
                with pe.Fori(0, 2) as j:
                    for k in range(3):
                        ssd_step(g, j, k, 0, (g, j, k + 1) if k < 2 else (g, j + 1, 0))
                for k in range(3):
                    ssd_step(g, 2, k, 6 + k, (g, 2, k + 1) if k < 2 else None if last else (g + 1, 0, 0))

            ssd_tokens(0, 0, 0)
            with pe.Fori(0, GROUPS - 1) as g:
                group(g, False)
            group(GROUPS - 1, True)
            def group_sum(g):
                pe.wait_ge(ysq_ready, 4 * g + 4)
                if g:
                    pe.wait_ge(rms_vec, 2 * g)
                for c in range(NCH):
                    L = CH if c < NCH - 1 else DEC
                    for f in range(4):
                        e = pe.matmul(PS[0:L, 3, c:c + 1], ysq[:, f, c * CH:c * CH + L], ones[:, 0:1],
                                      start=(f == 0), stop=(f == 3))
                e.then_inc(gs_mm, 1)

            def spread_rms(g):
                pe.wait_ge(rms_pow, 2 * g + 2)
                if g:
                    pe.wait_ge(yn_ready, 4 * g)
                for c in range(NCH):
                    L = CH if c < NCH - 1 else DEC
                    e = pe.matmul(PS[:, 4 + c // 4, (c % 4) * CH:(c % 4) * CH + L],
                                  rms_g[0:L, c:c + 1].broadcast_to([L, P]), ident[0:L, 0:L], start=True, stop=True)
                e.then_inc(rms_wide, 1)

            group_sum(0)
            pe.wait_ge(yg_ready, NCH * GROUPS + 3)
            spread_rms(0)
            pe.wait_ge(edge_v, 2 * GROUPS)
            for q in range(2):
                e = pe.transpose(PS[0:3 * CT, 7, q * P:(q + 1) * P], conv_tail[:, q, :, :], ident[:, :])
            e.then_inc(tails_t, 1)

            for g in range(GROUPS):
                pe.wait_ge(yb_lo, 4 * g + 4)
                for q in range(4):
                    v = q % 2
                    unit_ready(U_B + 4 * g + q)
                    for m in range(2):
                        thirds("brb", 24 * g + 6 * q + 3 * m, v,
                               [(cols(v, k, 256, m * P), tile_of(act_a, 4 * (g % 2) + k)) for k in range(4)])
                    if q == 0 and g < GROUPS - 1:
                        group_sum(g + 1)
                    if q == 1 and g < GROUPS - 1:
                        spread_rms(g + 1)
            for gi in range(GROUPS):
                v = gi // 2
                if gi % 2 == 0:
                    unit_ready(U_POOL + v)
                pe.wait_ge(pm_l, 2 * gi + 2)
                for m in range(2):
                    thirds("pool", 6 * gi + 3 * m, v,
                           [(cols(v, 2 * (gi % 2) + k, 256, m * P), tile_of(pooled[gi % 2], k)) for k in range(2)])
            pe.wait_ge(pl_vec, PL_DONE[-1])
            for q in range(2):
                e = pe.transpose(PS[0:PW * KT, 7, q * P:(q + 1) * P], pool_tail[:, q, :, :], ident[:, :])
            e.then_inc(ptail_t, 1)
            pe.wait_ge(mods_ready, 8)
            pe.wait_ge(ptail_v, 2)
            for s_ in range(2):
                for f in range(KT):
                    e = pe.matmul(PS[:, 4 + 2 * s_ + f // 4, (f % 4) * P:(f % 4 + 1) * P],
                                  mods[:, GATE1 + f, s_:s_ + 1].broadcast_to([P, P]), ident[:, :], start=True, stop=True)
            e.then_inc(gates_wide, 1)
            pe.wait_ge(mm_free["pool"], 3 * KT + 3)
            with pe.Fori(0, 4) as i:
                for v in range(2):
                    full_unit("bra", i * 2 + v + U_A, (i * 2 + v) * 3, v, act_b)
            def out_tile(t):
                L = CH if t < NCH - 1 else DEC
                if t >= 2:
                    pe.wait_ge(mm_free["out"], t - 1)
                for k in range(KT):
                    if t == 0:
                        pe.wait_ge(mg_lo, max(k, 3) + 1)
                        if k % 4 == 0:
                            pe.wait_ge(lo_ready, U_OUT + k + 4)
                    for a, b in PASSES:
                        for h in range(2):
                            e = pe.matmul(PS[0:L, 2 * (t % 2) + h, :], act_b[b][:, k, t * CH:t * CH + L],
                                          wo_res[k // 4][a][:, k % 4, h * 512:(h + 1) * 512],
                                          start=(k == 0 and a == b == 0), stop=(k == KT - 1 and a == 1))
                e.then_inc(mm["out"], 1)

            out_tile(0)
            for t in range(1, NCH):
                out_tile(t)
                turn(n2, xn[(t - 1) % 2][:, :, :], (t - 1) % 2, t - 1, 4 + 2 * ((t - 1) % 2), CH)
            turn(n2, xn[0][:, :, :], 0, NCH - 1, 4, DEC)

            def f_unit(u, v, sub0, wait):
                unit_ready(u)
                for n, (o, w) in enumerate(SUBS):
                    wait(n)
                    for k in range(KT):
                        for q, (a, b) in enumerate(PASSES):
                            e = pe.matmul(PS[:, n, 0:w], w_split[v][a][:, k * P:(k + 1) * P], act_b[b][:, k, o:o + w],
                                          start=(k == 0 and q == 0), stop=(k == KT - 1 and q == 2))
                    e.then_inc(mm["ffn"], 1)

            def gate_up(i, q, u, dve):
                f_unit(u, 0, None, lambda n: pe.wait_ge(mm_free["ffn"], dve + n + 1))
                f_unit(u + 1, 1, None, lambda n: pe.wait_ge(f_silu, (i * 2 + q) * 3 + n + 1))

            def down(u, dve, v):
                unit_ready(u + v)
                for m in range(4):
                    for n, (o, w) in enumerate(SUBS):
                        pe.wait_ge(mm_free["ffn"], dve + 12 * v + 3 * m + n + 1)
                        for k in range(2):
                            for q, (a, b) in enumerate(PASSES):
                                e = pe.matmul(PS[:, n, 0:w], w_split[v][a][:, k * 512 + m * P:k * 512 + (m + 1) * P],
                                              f_split[b][:, k, o:o + w],
                                              start=(k == 0 and q == 0), stop=(k == 1 and q == 2))
                        e.then_inc(mm["ffn"], 1)

            def first_gate(n):
                pe.wait_ge(n2.lo, 3 * n + 3)
                pe.wait_ge(mm_free["ffn"], n + 1)

            f_unit(U_FFN, 0, None, first_gate)
            f_unit(U_FFN + 1, 1, None, lambda n: pe.wait_ge(f_silu, n + 1))
            gate_up(0, 1, U_FFN + 2, 3)
            with pe.Fori(1, FG) as i:
                u0, dve0 = i * 6 + (U_FFN - 2), i * 30 - 24
                gate_up(i, 0, u0, dve0)
                pe.wait_ge(f_lo, i * 2)
                for v in range(2):
                    down(u0 + 2, dve0 + 3, v)
                gate_up(i, 1, u0 + 4, dve0 + 27)
            pe.wait_ge(f_lo, 2 * FG)
            for v in range(2):
                down(U_END - 2, FFN_DVE - 24, v)

            pe.wait_ge(mm_free["ffn"], FFN_DVE + 3)
            for t in range(NCH):
                L = CH if t < NCH - 1 else DEC
                if t >= 2:
                    pe.wait_ge(n3.added, t - 1)
                for f in range(KT):
                    e = pe.transpose(banks2(4 + 2 * (t % 2))[0:L, f, :], acc[:, f, t * CH:t * CH + L], ident[:, :])
                e.then_inc(n3.turned_in, 1)

        @block.vector
        def _(dve):
            def lo(u, v):
                dve.wait_ge(hi_ready, u + 1)
                dve.tensor_tensor(w_split[v][1][:, :], w_raw[v][:, :], w_split[v][0][:, :].bitcast(F32), ALU.subtract)\
                   .then_inc(lo_ready, 1)

            def lo_out(k):
                dve.wait_ge(hi_ready, U_OUT + k + 1)
                hi_, lo_ = wo_res[k // 4]
                dve.tensor_tensor(lo_[:, k % 4, :], w_raw[k % 2][:, :], hi_[:, k % 4, :].bitcast(F32), ALU.subtract)\
                   .then_inc(lo_ready, 1)

            dve.wait_ge(rows_t, 1)
            for q, (c_, n) in enumerate([(cols_conv, 5 * CT), (cols_vec, 104), (cols_hist, 3 * CT), (cols_pool, PW * KT)]):
                dve.tensor_copy(c_[:, :], PS[:, 6, q * P:q * P + n]).then_inc(cols_ready, 1)
            dve.wait_ge(c_ready, 2)
            dve.tensor_scalar(bc_head[:, 1, :], bc_head[:, 1, :], -1.0, None, ALU.mult).then_inc(cols_ready, 1)

            def mods_part(a, b):
                for s_ in range(2):
                    dve.tensor_tensor(mods[:, a:b, s_], PS[:, 7, 2 * a:2 * b].rearrange("p (t s) -> p t s", s=2)[:, :, s_],
                                      cols_vec[:, a:b], ALU.add).then_inc(mods_ready, 1)

            def gains(ln, scale_at, w_at, count):
                dve.wait_ge(mods_ready, count)
                for s_ in range(2):
                    dve.scalar_tensor_tensor(gain[:, ln, s_, :], mods[:, scale_at:scale_at + KT, s_], 1.0,
                                             cols_vec[:, w_at:w_at + KT], ALU.add, ALU.mult).then_inc(mods_ready, 1)

            def variance(n, t, v, L=P):
                dve.wait_ge(n.squared, t + 1)
                dve.tensor_scalar(small[0:L, 2 + v:3 + v], small[0:L, v:v + 1], 1.0 / D, EPS, ALU.mult, ALU.add)\
                   .then_inc(n.var, 1)

            def sum_slab(n, slot, src):
                for k in range(KT):
                    for s_ in range(2):
                        dst, c_ = ada_sum[:, slot, s_, :], silu_c[:, k, s_:s_ + 1]
                        if k == 0:
                            dve.tensor_scalar(dst, src[:, k, :], c_, None, ALU.mult).then_inc(ada_used, 1)
                        else:
                            dve.wait_ge(ada_used, n * 16 + 2 * k + s_ - 1)
                            dve.scalar_tensor_tensor(dst, src[:, k, :], c_, dst, ALU.mult, ALU.add).then_inc(ada_used, 1)

            variance(n1, 0, 0)
            for n, k in enumerate(ADA_SUMMED):
                dve.wait_ge(ada_first_in[k // 2], 32)
                sum_slab(n, n, ada_first[k])
            lo(0, 0)
            dve.wait_ge(wdt_h, 1)
            dve.tensor_tensor(wdt[1][:, :], wdt_raw[:, :], wdt[0][:, :].bitcast(F32), ALU.subtract).then_inc(wdt_l, 1)
            dve.wait_ge(mods_mm, ADA_DVE + 1)
            dve.wait_ge(cols_ready, 5)
            mods_part(0, 2 * KT)
            gains(0, SCALE1, 48, 2)

            def modulate(n, ln, shift, dst, t, v, b, s_, L):
                dve.wait_ge(n.turned, t + 1)
                for f in range(KT):
                    e = dve.tensor_scalar(dst[:, f, 0:L], banks2(b)[:, f, 0:L], gain[:, ln, s_, f:f + 1],
                                          mods[:, shift + f, s_:s_ + 1], ALU.mult, ALU.add)
                e.then_inc(n.modulated, 1)

            def low_part(n, src, act_, t, v, L):
                dve.wait_ge(n.hi, t + 1)
                tok = ds(t * P, L)
                dve.tensor_tensor(act_[1][:, :, tok], src[:, :, 0:L], act_[0][:, :, tok].bitcast(F32), ALU.subtract)\
                   .then_inc(n.lo, 1)

            def pairs(body):
                with dve.Fori(0, 4) as i:
                    body([(i * 2, 0, i), (i * 2 + 1, 1, i)], CH, 0)
                body([(8, 0, 4)], DEC, 1)

            def norm1_step(t, v, L=CH):
                modulate(n1, 0, SHIFT1, hf[1 - v], t - 1, 1 - v, 2 + 2 * (1 - v), 0, CH)
                variance(n1, t, v, L)
                low_part(n1, hf[1 - v], act_a, t - 1, 1 - v, CH)

            dve.sem_inc(n1.modulated, 2)
            dve.wait_ge(mods_ready, 4)
            with dve.Fori(0, 3) as i:
                norm1_step(i * 2 + 1, 1)
                norm1_step(i * 2 + 2, 0)
            norm1_step(7, 1)
            norm1_step(8, 0, DEC)
            modulate(n1, 0, SHIFT1, hf[0], 8, 0, 2, 1, DEC)
            low_part(n1, hf[0], act_a, 8, 0, DEC)

            steps = [0]

            def chain(e):
                steps[0] += 1
                e.then_inc(dt_vec, 1)
                dve.wait_ge(dt_vec, steps[0])

            dve.wait_ge(dt_tok, 1)
            dve.wait_ge(consts, N_MEMSET)
            bias = bc_head[:, 0, :]
            chain(dve.tensor_tensor(dt_in[:, 0:8, :], PS[:, 5, 0:8 * HEADS].rearrange("p (c h) -> p c h", h=HEADS),
                                    bias.unsqueeze(1).broadcast_to([P, 8, HEADS]), ALU.add))
            chain(dve.tensor_tensor(dt_in[0:DEC, 8, :], PS[0:DEC, 5, 8 * HEADS:9 * HEADS], bc_head[0:DEC, 0, :], ALU.add))
            dve.wait_ge(dt_act, 2)
            chain(dve.tensor_scalar(dt_s[:, :, :], dt_e[:, :, :], 2.0, None, ALU.add))
            chain(dve.reciprocal(dt_q[:, :, :], dt_s[:, :, :]))
            chain(dve.tensor_tensor(dt_s[:, :, :], dt_e[:, :, :], dt_q[:, :, :], ALU.mult))
            chain(dve.tensor_tensor(dt_q[:, :, :], dt_s[:, :, :], dt_s[:, :, :], ALU.mult))
            chain(dve.tensor_scalar(dt_p[:, :, :], dt_q[:, :, :], POLY[8], None, ALU.mult))
            for k in range(7, 0, -1):
                chain(dve.scalar_tensor_tensor(dt_p[:, :, :], dt_p[:, :, :], POLY[k], dt_q[:, :, :], ALU.add, ALU.mult))
            chain(dve.scalar_tensor_tensor(dt_p[:, :, :], dt_p[:, :, :], 1.0, dt_s[:, :, :], ALU.add, ALU.mult))
            chain(dve.tensor_scalar(dt_in[:, :, :], dt_in[:, :, :], 0.0, None, ALU.max))
            chain(dve.scalar_tensor_tensor(dt_tab[:, :, :], dt_p[:, :, :], 2.0, dt_in[:, :, :], ALU.mult, ALU.add))
            chain(dve.memset(dt_tab[DEC:P, 8, :], 0.0))
            chain(dve.tensor_tensor(dt_q[:, :, :], dt_tab[:, :, :], bc_head[:, 1, :].unsqueeze(1)
                                    .broadcast_to([P, NCH, HEADS]), ALU.mult))
            assert steps[0] == DV_DTA
            with dve.Fori(0, 8) as i:
                for v in range(2):
                    u = i * 2 + v
                    lo(u + 1, 1 - v)
                    dve.wait_ge(ada_in[v], i * 16 + 16)
                    dve.wait_ge(mods_mm, u + ADA_DVE - 1)
                    sum_slab(u + ADA_DVE, v, ada[v])
            dve.wait_ge(dt_cum, 1)
            ps5 = PS[:, 5, 0:NCH * HEADS].rearrange("p (c h) -> p c h", h=HEADS)
            ps6 = PS[:, 6, 0:NCH * HEADS].rearrange("p (c h) -> p c h", h=HEADS)
            chain(dve.tensor_copy(dt_s[:, :, :], ps5))
            chain(dve.tensor_copy(dt_p[:, :, :], ps6))
            chain(dve.tensor_scalar(nacs_tab[:, :, :], dt_s[:, :, :], -1.0, None, ALU.mult))
            chain(dve.tensor_tensor(dt_e[:, :, :], dt_p[:, :, :], dt_s[:, :, :], ALU.subtract))
            chain(dve.tensor_copy(acs_row[:, 0:1024].rearrange("h (b l) -> h b l", b=2), PS[0:HEADS, 3:5, :]))
            chain(dve.tensor_copy(acs_row[:, 1024:1152], PS[0:HEADS, 6, 384:512]))
            assert steps[0] == DV_TAB - 1
            chain(dve.memset(small[:, 6:8], 0.0))
            dve.wait_ge(mods_mm, ADA_DVE + 17)
            mods_part(2 * KT, 48)
            gains(1, SCALE2, 56, 6)

            dve.sem_inc(cv_step, 8)
            with dve.Fori(0, 12) as i:
                for v in range(2):
                    n_ = i * 2 + v
                    lo(n_ + 17, 1 - v)
                    hist = cols_hist[:, :].rearrange("p (k t) -> p k t", k=3)
                    dve.wait_ge(cv_step, n_ * 4 + 4)
                    dve.tensor_copy(raw[v][:, 3 + SEQ:6 + SEQ], hist[:, :, ds(n_, 1)].rearrange("p k o -> p (k o)"))\
                       .then_inc(raw_hist, 1)
                    dve.wait_ge(raw_hist, n_ + 1)
                    dve.wait_ge(mm_free["xbc"], n_ * 3 + 6)
                    dve.tensor_copy(conv_tail[:, :, :, ds(n_, 1)].rearrange("p s k o -> p s (k o)"),
                                    raw[v][:, SEQ:SEQ + 2 * (DEC + 3)].rearrange("p (s k) -> p s k", s=2)[:, :, 0:3])
                    dve.wait_ge(cv_store[v], i * 32)
                    for k in range(4):
                        tap = cols_conv[:, ds(n_ + k * CT, 1)]
                        if k:
                            dve.wait_ge(cv_step, n_ * 4 + k + 8)
                            dve.scalar_tensor_tensor(cv[v][:, 0:T + 3], raw[v][:, k:k + T + 3], tap, cv[v][:, 0:T + 3],
                                                     ALU.mult, ALU.add).then_inc(cv_step, 1)
                        else:
                            dve.tensor_scalar(cv[v][:, 0:T + 3], raw[v][:, 0:T + 3], tap,
                                              cols_conv[:, ds(n_ + 4 * CT, 1)], ALU.mult, ALU.add).then_inc(cv_step, 1)

            def tokens_of(ap):
                return ap.rearrange("p (h d) -> p h d", d=HD)

            def head_col(tab, g, j, k):
                t_ = tab[:, :, :].rearrange("p c h -> p (c h)")
                return t_[:, ds((j * 3 + k) * HEADS + g * HPG, HPG)].unsqueeze(2).broadcast_to([P, HPG, HD])

            def chunk_operands(g, j, k):
                t = g * NCH + j * 3 + k
                dve.wait_ge(ssd_a, t + 1)
                dve.tensor_tensor(x_dt[:, :, :], tokens_of(bank(3)), head_col(dt_tab, g, j, k), ALU.mult).then_inc(v_x, 1)
                dve.tensor_copy(b_tok[:, :], PS[:, 4, 0:NS]).then_inc(v_b, 1)
                dve.tensor_tensor(skip[:, :, :], tokens_of(bank(3)),
                                  bc_head[:, 2, :][:, ds(g * HPG, HPG)].unsqueeze(2).broadcast_to([P, HPG, HD]), ALU.mult)\
                   .then_inc(v_skip, 1)
                dve.wait_ge(v_x, t + 1)
                dve.tensor_tensor(x_end[:, :, :], x_dt[:, :, :], head_col(dend_tab, g, j, k), ALU.mult).then_inc(v_xend, 1)
                dve.wait_ge(decay_ready, t + 1)
                dve.tensor_tensor(mix[:, :, :], decay[:, :, :], PS[:, 4, P:2 * P].unsqueeze(1).broadcast_to([P, HPG, CH]),
                                  ALU.mult).then_inc(v_mix, 1)

            def ssd_step(g, j, k, c, ahead):
                t = g * NCH + j * 3 + k
                dve.wait_ge(ssd_b, t + 1)
                dve.tensor_tensor(y_tok[:, :, :], tokens_of(bank(6)), head_col(eacs_tab, g, j, k), ALU.mult).then_inc(v_y0, 1)
                dve.wait_ge(v_y0, t + 1)
                dve.tensor_tensor(y_tok[:, :, :], tokens_of(bank(5)), y_tok[:, :, :], ALU.add).then_inc(v_y1, 1)
                dve.wait_ge(v_y1, t + 1)
                dve.wait_ge(v_skip, t + 1)
                dve.tensor_tensor(y_tok[:, :, :], y_tok[:, :, :], skip[:, :, :], ALU.add).then_inc(y_ready, 1)
                dve.wait_ge(state_ready, g * 11 + (j * 3 + k + 1 if c < 8 else 10))
                dve.tensor_tensor(state[:, :, :], state[:, :, :], head_col(bdec_tab, g, j, k), ALU.mult).then_inc(v_s0, 1)
                dve.wait_ge(v_s0, t + 1)
                dve.tensor_tensor(state[:, :, :], tokens_of(bank(7)), state[:, :, :], ALU.add).then_inc(state_ready, 1)
                if ahead:
                    chunk_operands(*ahead)
                dve.wait_ge(y_store[k], (g * 3 + j) * 16)
                dve.wait_ge(ssd_c, t + 1)
                dve.tensor_tensor(yg[k][:, :, :], bank(6).rearrange("p (f l) -> p f l", f=4), z_in[k][:, :, :], ALU.mult)\
                   .then_inc(yg_ready, 1)
                if c == NCH - 2:
                    dve.wait_ge(edge_t, g * 3 + 1)
                    dve.wait_ge(edge_store[0], g * 16)
                    dve.tensor_copy(state_out[0][:, :, :], bank(7).rearrange("p (f n) -> p f n", f=4)).then_inc(edge_v, 1)
                    dve.wait_ge(edge_t, g * 3 + 2)
                    dve.tensor_copy(state[:, :, :], tokens_of(bank(5))).then_inc(state_ready, 1)
                if c == NCH - 1:
                    dve.wait_ge(edge_t, g * 3 + 3)
                    dve.wait_ge(edge_store[1], g * 16)
                    dve.tensor_copy(state_out[1][:, :, :], bank(7).rearrange("p (f n) -> p f n", f=4)).then_inc(edge_v, 1)
                    if ahead:
                        dve.memset(state[:, :, :], 0.0).then_inc(state_ready, 1)

            def group(g, last):
                with dve.Fori(0, 2) as j:
                    lo((g * 3 + j) * 2 + U_SSD + 1, 1)
                    for k in range(3):
                        ssd_step(g, j, k, 0, (g, j, k + 1) if k < 2 else (g, j + 1, 0))
                        if k == 1:
                            lo((g * 3 + j) * 2 + U_SSD + 2, 0)
                lo((g * 3 + 2) * 2 + U_SSD + 1, 1)
                for k in range(3):
                    ssd_step(g, 2, k, 6 + k, (g, 2, k + 1) if k < 2 else None if last else (g + 1, 0, 0))
                    if k == 1:
                        lo((g * 3 + 2) * 2 + U_SSD + 2, 0)

            dve.sem_inc(yg_ready, 3)
            dve.wait_ge(dt_act, 5)
            dve.wait_ge(cv_silu, CT)
            for q in range(2):
                dve.wait_ge(cv_store[q], 12 * 32)
                dve.wait_ge(z_store[q], 8 * 32)
            dve.wait_ge(acs_out, 16 * GROUPS)
            dve.memset(state[:, :, :], 0.0).then_inc(state_ready, 1)
            chunk_operands(0, 0, 0)
            with dve.Fori(0, GROUPS - 1) as g:
                group(g, False)
            group(GROUPS - 1, True)

            def group_variance(g):
                if g:
                    dve.wait_ge(rms_pow, 2 * g)
                dve.wait_ge(gs_mm, g + 1)
                for r, c in [(P, slice(0, NCH - 1)), (DEC, slice(NCH - 1, NCH))]:
                    dve.tensor_scalar(rms_v[0:r, c], PS[0:r, 3, c], 1.0 / 512, EPS, ALU.mult, ALU.add).then_inc(rms_vec, 1)

            def y_norm(g, f):
                v = g % 2
                dve.wait_ge(rms_wide, g + 1)
                dve.scalar_tensor_tensor(y_in[v][:, f, :], y_in[v][:, f, :], cols_vec[:, 72 + 4 * g + f:73 + 4 * g + f],
                                         PS[:, 4:7, :].rearrange("p b l -> p (b l)")[:, 0:T], ALU.mult, ALU.mult)\
                   .then_inc(yn_ready, 1)

            def y_low(g, f):
                v = g % 2
                dve.wait_ge(yb_hi, 4 * g + f + 1)
                dve.tensor_tensor(act_a[1][:, 4 * v + f, :], y_in[v][:, f, :],
                                  act_a[0][:, 4 * v + f, :].bitcast(F32), ALU.subtract).then_inc(yb_lo, 1)

            dve.wait_ge(mm_free["ssd"], 75)
            dve.sem_inc(mm_free["brb"], 3)
            group_variance(0)
            for f in range(4):
                y_norm(0, f)
                if f:
                    y_low(0, f - 1)
            y_low(0, 3)
            for q in range(2):
                dve.wait_ge(edge_store[q], 16 * GROUPS)
                dve.wait_ge(gp_store[q], 12 * 16)
            for k in range(3):
                dve.wait_ge(y_store[k], 12 * 16)
            dve.wait_ge(tails_t, 1)
            dve.tensor_copy(tail_rows[:, :, :], PS[0:3 * CT, 7, 0:2 * P].rearrange("p (q c) -> p q c", q=2))\
               .then_inc(tails_v, 2)
            at_p, at_s = PW, SEQ + 2 * PW
            full = at_s + DEC
            count = [0]

            def pstep(e):
                count[0] += 1
                e.then_inc(pl_vec, 1)
                dve.wait_ge(pl_vec, count[0])

            def window_sums(j):
                dve.wait_ge(pool_x_in, 32 * (j + 1))
                if j:
                    dve.wait_ge(pl_store, 32 * j)
                pstep(dve.tensor_copy(pool_x[:, at_s - PW:at_s], cols_pool[:, :].rearrange("p (r t) -> p r t", t=KT)[:, :, j]))
                pstep(dve.tensor_copy(pool_tail[:, 0, :, j], pool_x[:, at_p + SEQ - PW:at_p + SEQ]))
                pstep(dve.tensor_copy(pool_tail[:, 1, :, j], pool_x[:, full - PW:full]))
                cur, first = pool_x, 0
                for k in range(j // 2 + 1):
                    nxt, first = [pool_s0, pool_s1][k % 2], first + (1 << k)
                    pstep(dve.tensor_tensor(nxt[:, first:full], cur[:, first:full], cur[:, first - (1 << k):full - (1 << k)],
                                            ALU.add))
                    cur = nxt

            def means(j):
                w_, cur, x = 2 << (j // 2), [pool_s0, pool_s1][(j // 2) % 2], pool_x
                head, rest = slice(at_p, at_p + w_ - 1), slice(at_p + w_ - 1, at_p + SEQ)
                pstep(dve.tensor_tensor(cur[:, head], cur[:, head], inv_pos[:, 0:w_ - 1], ALU.mult))
                pstep(dve.tensor_tensor(cur[:, head], cur[:, head], x[:, head], ALU.subtract))
                for r in (rest, slice(at_s, full)):
                    pstep(dve.scalar_tensor_tensor(cur[:, r], cur[:, r], 1.0 / w_, x[:, r], ALU.mult, ALU.subtract))
                assert count[0] == PL_DONE[j]

            dve.memset(pool_x[:, 0:PW], 0.0).then_inc(pl_set, 1)
            dve.wait_ge(pl_set, 1)
            for g in range(GROUPS):
                for q in range(4):
                    lo(U_B + 4 * g + q + 1, 1 - q % 2)
                    for m in range(2):
                        s0 = 24 * g + 6 * q + 3 * m
                        for n, (o, w) in enumerate(SUBS):
                            dve.wait_ge(mm["brb"], s0 + n + 1)
                            dst = acc[:, 2 * q + m, o:o + w]
                            if g == 0:
                                dve.tensor_copy(dst, PS[:, n, 0:w]).then_inc(mm_free["brb"], 1)
                            else:
                                dve.wait_ge(mm_free["brb"], s0 + n - 20)
                                dve.tensor_tensor(dst, PS[:, n, 0:w], dst, ALU.add).then_inc(mm_free["brb"], 1)
                        piece = 2 * q + m
                        if piece in (0, 3):
                            window_sums(2 * g + piece // 3)
                        if piece in (1, 4):
                            means(2 * g + piece // 4)
                        if g < GROUPS - 1 and piece == 2:
                            group_variance(g + 1)
                        if g < GROUPS - 1 and 3 <= piece < 7:
                            y_norm(g + 1, piece - 3)
                        if g < GROUPS - 1 and piece > 3:
                            y_low(g + 1, piece - 4)

            dve.sem_inc(mm_free["pool"], 3)

            def pooled_parts(gi):
                for m in range(2):
                    dve.wait_ge(pm_h, 2 * gi + m + 1)
                    hi_, lo_ = pooled[gi % 2]
                    dve.tensor_tensor(lo_[:, m, :], pooled_in[gi][:, m, :], hi_[:, m, :].bitcast(F32), ALU.subtract)\
                       .then_inc(pm_l, 1)

            def a_lows(gi):
                for m in range(2):
                    j = 2 * gi + m
                    for n, (o, w) in enumerate(SUBS):
                        dve.wait_ge(ab_hi, 3 * j + n + 1)
                        dve.scalar_tensor_tensor(act_b[1][:, j, o:o + w], PS[:, n, 0:w], cols_vec[:, 64 + j:65 + j],
                                                 act_b[0][:, j, o:o + w].bitcast(F32), ALU.mult, ALU.subtract)\
                           .then_inc(mm_free["pool"], 1)

            lo(U_POOL + 1, 1)
            pooled_parts(0)
            for gi in range(GROUPS):
                if gi == 2:
                    lo(U_A, 0)
                if gi < GROUPS - 1:
                    pooled_parts(gi + 1)
                a_lows(gi)
            dve.wait_ge(ptail_t, 1)
            dve.tensor_copy(pool_rows[:, :, :], PS[0:PW * KT, 7, 0:2 * P].rearrange("p (q c) -> p q c", q=2))\
               .then_inc(ptail_v, 2)

            dve.sem_inc(mm_free["bra"], 3)
            dve.sem_inc(mg_vec, 5)
            def merge_tile(m, v):
                dve.wait_ge(gate_tanh, m * 2 + 2)
                dve.wait_ge(mg_vec, m * 5 + 5)
                for n, (o, w) in enumerate(SUBS):
                    dve.wait_ge(mm["bra"], m * 3 + n + 1)
                    dve.scalar_tensor_tensor(mg_t[:, o:o + w], gates[v][0][:, o:o + w], 1.0, PS[:, n, 0:w],
                                             ALU.add, ALU.mult).then_inc(mm_free["bra"], 1)
                row = acc[:, ds(m, 1), :].rearrange("p o t -> p (o t)")
                dve.scalar_tensor_tensor(gates[v][1][:, :], gates[v][1][:, :], 1.0, row, ALU.add, ALU.mult)\
                   .then_inc(mg_vec, 4)
                dve.wait_ge(mg_vec, m * 5 + 9)
                dve.wait_ge(mm_free["bra"], m * 3 + 6)
                dve.tensor_tensor(row, mg_t[:, :], gates[v][1][:, :], ALU.add).then_inc(mg_vec, 1)

            with dve.Fori(0, 3) as i:
                for v in range(2):
                    lo(i * 2 + v + U_A + 1, 1 - v)
                    merge_tile(i * 2 + v, v)
            lo(U_A + 7, 1)
            merge_tile(6, 0)
            for k in range(4):
                lo_out(k)
            merge_tile(7, 1)
            for m in range(KT):
                dve.wait_ge(mg_hi, m + 1)
                dve.scalar_tensor_tensor(act_b[1][:, m, :], acc[:, m, :], 0.5, act_b[0][:, m, :].bitcast(F32),
                                         ALU.mult, ALU.subtract).then_inc(mg_lo, 1)
            for k in range(4, KT):
                lo_out(k)
            lo(U_FFN, 0)

            def norm2_add(t, v, s_, L):
                dve.wait_ge(mm["out"], t + 1)
                dve.tensor_tensor(xn[v][0:L, :, :].rearrange("t f c -> t (f c)"),
                                  PS[0:L, 2 * v:2 * v + 2, :].rearrange("t b c -> t (b c)"), gate_row[0:L, s_, :], ALU.mult)\
                   .then_inc(mm_free["out"], 1)
                dve.wait_ge(n2.landed[v], (t - v) * 8 + 16)
                dve.wait_ge(mm_free["out"], t + 1)
                dve.tensor_tensor(xr[v][0:L, :, :], xn[v][0:L, :, :], xr[v][0:L, :, :], ALU.add).then_inc(n2.added, 1)

            def norm2_step(t, v, s_=0, L=CH):
                norm2_add(t, v, s_, L)
                modulate(n2, 1, SHIFT2, h2[1 - v], t - 1, 1 - v, 4 + 2 * (1 - v), 0, CH)
                variance(n2, t, v, L)
                low_part(n2, h2[1 - v], act_b, t - 1, 1 - v, CH)

            dve.sem_inc(n2.modulated, 2)
            dve.wait_ge(gates_row, 1)
            norm2_add(0, 0, 0, CH)
            variance(n2, 0, 0)
            with dve.Fori(0, 3) as i:
                norm2_step(i * 2 + 1, 1)
                norm2_step(i * 2 + 2, 0)
            norm2_step(7, 1)
            norm2_step(8, 0, 1, DEC)
            dve.sem_inc(mm_free["ffn"], 3)
            modulate(n2, 1, SHIFT2, h2[0], 8, 0, 4, 1, DEC)
            low_part(n2, h2[0], act_b, 8, 0, DEC)

            for q in range(2):
                dve.wait_ge(x2_out[q], 16 * (5 - q))
            dve.wait_ge(y_add, 1)

            def product(i, q, sub0):
                dve.wait_ge(f_lo, i * 2 + q)
                for n, (o, w) in enumerate(SUBS):
                    dve.wait_ge(f_silu, (i * 2 + q) * 3 + n + 1)
                    dve.wait_ge(mm["ffn"], sub0 + n + 1)
                    dve.tensor_tensor(f_val[:, o:o + w], PS[:, n, 0:w], silu_g[:, o:o + w], ALU.mult)\
                       .then_inc(mm_free["ffn"], 1)

            def f_low(i, q):
                dve.wait_ge(f_hi, i * 2 + q + 1)
                dve.tensor_tensor(f_split[1][:, q, :], f_val[:, :], f_split[0][:, q, :].bitcast(F32), ALU.subtract)\
                   .then_inc(f_lo, 1)

            def sums(v, sub0, dve0):
                for m in range(4):
                    for n, (o, w) in enumerate(SUBS):
                        s_ = 3 * m + n
                        dve.wait_ge(mm["ffn"], sub0 + s_ + 1)
                        f = 4 * v + m
                        parts = [(o, w, 0)] if o + w <= SEQ else [(o, SEQ - o, 0), (SEQ, DEC, 1)]
                        for at_, n_, q in parts:
                            dst = acc[:, f, at_:at_ + n_]
                            e = dve.scalar_tensor_tensor(dst, PS[:, n, at_ - o:at_ - o + n_], mods[:, GATE2 + f, q:q + 1], dst,
                                                         ALU.mult, ALU.add)
                        e.then_inc(mm_free["ffn"], 1)

            lo(U_FFN + 1, 1)
            lo(U_FFN + 2, 0)
            product(0, 0, 3)
            lo(U_FFN + 3, 1)
            f_low(0, 0)
            lo(U_FFN + 4, 0)
            product(0, 1, 9)
            with dve.Fori(1, FG) as i:
                u0, sub0, dve0 = i * 6 + (U_FFN - 2), i * 36 - 24, i * 30 - 24
                f_low(i - 1, 1)
                lo(u0 + 1, 1)
                lo(u0 + 2, 0)
                product(i, 0, sub0 + 3)
                lo(u0 + 3, 1)
                dve.wait_ge(mm_free["ffn"], dve0)
                sums(0, sub0 + 6, dve0 + 3)
                lo(u0 + 4, 0)
                sums(1, sub0 + 18, dve0 + 15)
                lo(u0 + 5, 1)
                f_low(i, 0)
                lo(u0 + 6, 0)
                product(i, 1, sub0 + 33)
            f_low(FG - 1, 1)
            lo(U_END - 1, 1)
            dve.wait_ge(mm_free["ffn"], FFN_DVE - 24)
            for v in range(2):
                sums(v, FFN_SUBS - 24 + 12 * v, FFN_DVE - 24 + 12 * v)

            def norm3_add(t, v, L=CH):
                dve.wait_ge(n3.landed[v], (t - v) * 8 + 16)
                dve.wait_ge(n3.turned_in, t + 1)
                dve.tensor_tensor(fx[v][0:L, :, :], banks2(4 + 2 * v)[0:L, :, :], fr[v][0:L, :, :], ALU.add)\
                   .then_inc(n3.added, 1)

            def norm3_scale(t, v, stored, L=CH):
                dve.wait_ge(n3.rms, t + 1)
                dve.wait_ge(out_sem[v], stored)
                dve.scalar_tensor_tensor(fo[v][0:L, :, :], fx[v][0:L, :, :], small[0:L, 4 + v:5 + v],
                                         final_w[0:L, :, :], ALU.mult, ALU.mult).then_inc(n3.scaled, 1)

            def norm3_step(t, v, stored, L=CH):
                dve.wait_ge(n3.scaled, t - 1)
                norm3_add(t, v, L)
                norm3_scale(t - 1, 1 - v, stored)
                variance(n3, t, v, L)

            dve.wait_ge(fw_in, 16)
            norm3_add(0, 0)
            variance(n3, 0, 0)
            with dve.Fori(0, 3) as i:
                norm3_step(i * 2 + 1, 1, i * 16)
                norm3_step(i * 2 + 2, 0, i * 16)
            norm3_step(7, 1, 48)
            norm3_step(8, 0, 48, DEC)
            norm3_scale(8, 0, 64, DEC)


_INS = ["x_prompt", "x_sample", "c_prompt", "c_sample", "state_pool", "state_conv", "state_ssm", "w_ada", "b_ada",
        "norm1_w", "norm2_w", "w_in", "pool_group_w", "pool_scale", "conv_w", "conv_b", "dt_bias", "a_log", "d_skip",
        "ssm_norm_w", "w_branch_a", "w_branch_b", "w_out", "w_ffn_gate", "w_ffn_up", "w_ffn_down", "final_norm_w"]
_OUTS = [(1, SEQ, D), (1, DEC, D), (1, 1, PW, D), (1, 1, 3, CONV), (1, 1, HEADS, HD, NS),
         (1, 1, PW, D), (1, 1, 3, CONV), (1, 1, HEADS, HD, NS)]


def kernel(**inputs):
    import numpy as np
    import concourse.bacc as bacc
    from concourse.bass_utils import run_bass_kernel_spmd

    nc = bacc.Bacc("TRN2", target_bir_lowering=False, num_devices=1)
    arrays, ins, outs = {}, {}, []
    for name in _INS:
        a = np.ascontiguousarray(inputs[name])
        arrays[f"in_{name}"] = a
        ins[name] = nc.dram_tensor(f"in_{name}", a.shape, mybir.dt.from_np(a.dtype), kind="ExternalInput").ap()
    for i, shape in enumerate(_OUTS):
        outs.append(nc.dram_tensor(f"out_{i}", shape, F32, kind="ExternalOutput").ap())
    build(nc, ins, outs)
    r = run_bass_kernel_spmd(nc, [arrays], core_ids=[0])
    return tuple(r.results[0][f"out_{i}"] for i in range(len(_OUTS)))
```
